# Optimizing a Trainium2 kernel written in Bass

```python
import math
import jax, jax.numpy as jnp
from jax import lax
import numpy as np

D_MODEL = 1024
BATCH = 1
SEQ = 256
DEPTH = 2

D_MIX = D_MODEL
CONV_DIM = D_MIX // 2
CONV_GROUPS = 8
CONV_WIDTH = 31
GLA_HEADS = 4
GLA_VAL_DIM = D_MIX // 2
GLA_HEAD_V = GLA_VAL_DIM // GLA_HEADS
GLA_KEY_DIM = GLA_VAL_DIM // 2
GLA_HEAD_K = GLA_KEY_DIM // GLA_HEADS
GATE_RANK = 16
GATE_TAU = 16.0
GLA_CHUNK = 64
IN_COLS = 2 * CONV_DIM + 2 * GLA_KEY_DIM + 2 * GLA_VAL_DIM + GATE_RANK
MEM_LEN = 256
X_HEADS = 4
X_HEAD_DIM = D_MODEL // X_HEADS
D_FF = int(math.ceil(8 * D_MODEL / 3 / 256) * 256)
DEEPNORM_ALPHA = (2 * DEPTH) ** 0.25
DEEPNORM_BETA = (8 * DEPTH) ** -0.25
LN_EPS = 1e-5


def layer_norm(x, g, b):
    xf = x.astype(jnp.float32)
    mu = jnp.mean(xf, axis=-1, keepdims=True)
    xc = xf - mu
    var = jnp.mean(xc * xc, axis=-1, keepdims=True)
    return (xc * lax.rsqrt(var + LN_EPS) * g.astype(jnp.float32) + b.astype(jnp.float32)).astype(x.dtype)

def rms_norm(x, g):
    xf = x.astype(jnp.float32)
    ms = jnp.mean(xf * xf, axis=-1, keepdims=True)
    return (xf * lax.rsqrt(ms + LN_EPS) * g.astype(jnp.float32)).astype(x.dtype)

def causal_depthwise_conv(u, w, b):
    c = u.shape[-1]
    y = lax.conv_general_dilated(
        u, w[:, None, :].astype(u.dtype), window_strides=(1,),
        padding=[(w.shape[0] - 1, 0)],
        dimension_numbers=("NWC", "WIO", "NWC"),
        feature_group_count=c)
    return y + b

def gla_chunked(q, k, v, log_a):
    out_dtype = v.dtype
    bsz, t, h, dk = q.shape
    dv = v.shape[-1]
    n = t // GLA_CHUNK

    def to_chunks(z):
        return z.astype(jnp.float32).reshape(bsz, n, GLA_CHUNK, h, z.shape[-1]).transpose(0, 3, 1, 2, 4)

    qc = to_chunks(q) * (dk ** -0.5)
    kc, vc, gc = to_chunks(k), to_chunks(v), to_chunks(log_a)
    bcum = jnp.cumsum(gc, axis=3)
    b_last = bcum[:, :, :, -1:, :]
    qe = qc * jnp.exp(bcum)
    ke = kc * jnp.exp(-bcum)
    kd = kc * jnp.exp(b_last - bcum)
    causal = jnp.tril(jnp.ones((GLA_CHUNK, GLA_CHUNK), dtype=bool))
    att = jnp.einsum("bhncd,bhnsd->bhncs", qe, ke)
    att = jnp.where(causal, att, 0.0)
    o_intra = jnp.einsum("bhncs,bhnse->bhnce", att, vc)
    upd = jnp.einsum("bhncd,bhnce->bhnde", kd, vc)
    decay = jnp.exp(b_last[:, :, :, 0, :])

    def step(state, inp):
        dec, u = inp
        return dec[..., None] * state + u, state

    s0 = jnp.zeros((bsz, h, dk, dv), jnp.float32)
    _, s_prev = lax.scan(step, s0, (jnp.moveaxis(decay, 2, 0), jnp.moveaxis(upd, 2, 0)))
    s_prev = jnp.moveaxis(s_prev, 0, 2)
    o_inter = jnp.einsum("bhncd,bhnde->bhnce", qe, s_prev)
    o = (o_intra + o_inter).transpose(0, 2, 3, 1, 4).reshape(bsz, t, h, dv)
    return o.astype(out_dtype)

def hybrid_mixer(h, w_in, w_a2, b_a, conv_w, conv_b, conv_ln_g, conv_ln_b, gla_norm_g, w_out):
    bsz, t, _ = h.shape
    proj = h @ w_in
    cuts = np.cumsum([CONV_DIM, CONV_DIM, GLA_KEY_DIM, GLA_KEY_DIM, GLA_VAL_DIM, GLA_VAL_DIM]).tolist()
    c_a, c_g, q, k, v, r, a_low = jnp.split(proj, cuts, axis=-1)
    u = c_a * jax.nn.sigmoid(c_g)
    u = causal_depthwise_conv(u, conv_w, conv_b)
    u = jax.nn.silu(layer_norm(u, conv_ln_g, conv_ln_b))
    z = a_low @ w_a2 + b_a
    log_a = jax.nn.log_sigmoid(z.astype(jnp.float32)) / GATE_TAU
    heads = lambda y, d: y.reshape(bsz, t, GLA_HEADS, d)
    o = gla_chunked(heads(q, GLA_HEAD_K), heads(k, GLA_HEAD_K), heads(v, GLA_HEAD_V),
                    heads(log_a, GLA_HEAD_K))
    o = rms_norm(o, gla_norm_g) * jax.nn.silu(heads(r, GLA_HEAD_V))
    o = o.reshape(bsz, t, GLA_VAL_DIM)
    return jnp.concatenate([u, o], axis=-1) @ w_out

def memory_cross_attention(x, mem, w_q, w_kv, w_o):
    bsz, t, _ = x.shape
    q = (x @ w_q).reshape(bsz, t, X_HEADS, X_HEAD_DIM)
    kv = mem @ w_kv
    k, v = jnp.split(kv, 2, axis=-1)
    k = k.reshape(bsz, MEM_LEN, X_HEADS, X_HEAD_DIM)
    v = v.reshape(bsz, MEM_LEN, X_HEADS, X_HEAD_DIM)
    s = jnp.einsum("bthd,bmhd->bhtm", q.astype(jnp.float32), k.astype(jnp.float32)) * (X_HEAD_DIM ** -0.5)
    p = jax.nn.softmax(s, axis=-1).astype(v.dtype)
    o = jnp.einsum("bhtm,bmhd->bthd", p, v).reshape(bsz, t, D_MODEL)
    return o @ w_o

def swiglu(x, w_in, w_out):
    g, u = jnp.split(x @ w_in, 2, axis=-1)
    return (jax.nn.silu(g) * u) @ w_out

def first_inputs(seed: int = 0) -> dict:
    key = jax.random.key(seed)
    ks = jax.random.split(key, 24)
    nrm = lambda k, shape, scale: jax.random.normal(k, shape, jnp.float32) * scale
    gain = lambda k, shape: 1.0 + nrm(k, shape, 0.02)
    L = DEPTH
    return {
        "x": nrm(ks[0], (BATCH, SEQ, D_MODEL), 1.0),
        "mem": nrm(ks[1], (BATCH, MEM_LEN, D_MODEL), 1.0),
        "ln0_g": gain(ks[2], (D_MODEL,)),
        "ln0_b": nrm(ks[3], (D_MODEL,), 0.02),
        "w_in": nrm(ks[4], (L, D_MODEL, IN_COLS), D_MODEL ** -0.5),
        "w_a2": nrm(ks[5], (L, GATE_RANK, GLA_KEY_DIM), GATE_RANK ** -0.5),
        "b_a": nrm(ks[6], (L, GLA_KEY_DIM), 0.01),
        "conv_w": nrm(ks[7], (L, CONV_WIDTH, CONV_DIM), CONV_WIDTH ** -0.5),
        "conv_b": nrm(ks[8], (L, CONV_DIM), 0.02),
        "conv_ln_g": gain(ks[9], (L, CONV_DIM)),
        "conv_ln_b": nrm(ks[10], (L, CONV_DIM), 0.02),
        "gla_norm_g": gain(ks[11], (L, GLA_HEAD_V)),
        "w_mix_out": nrm(ks[12], (L, D_MIX, D_MODEL), DEEPNORM_BETA * D_MIX ** -0.5),
        "ln1_g": gain(ks[13], (L, D_MODEL)),
        "ln1_b": nrm(ks[14], (L, D_MODEL), 0.02),
        "w_xq": nrm(ks[15], (L, D_MODEL, D_MODEL), D_MODEL ** -0.5),
        "w_xkv": jnp.concatenate([
            nrm(ks[16], (L, D_MODEL, D_MODEL), D_MODEL ** -0.5),
            nrm(jax.random.fold_in(ks[16], 1), (L, D_MODEL, D_MODEL), DEEPNORM_BETA * D_MODEL ** -0.5)], axis=-1),
        "w_xo": nrm(ks[17], (L, D_MODEL, D_MODEL), DEEPNORM_BETA * D_MODEL ** -0.5),
        "ln2_g": gain(ks[18], (L, D_MODEL)),
        "ln2_b": nrm(ks[19], (L, D_MODEL), 0.02),
        "w_ffn_in": nrm(ks[20], (L, D_MODEL, 2 * D_FF), D_MODEL ** -0.5),
        "w_ffn_out": nrm(ks[21], (L, D_FF, D_MODEL), DEEPNORM_BETA * D_FF ** -0.5),
        "ln3_g": gain(ks[22], (L, D_MODEL)),
        "ln3_b": nrm(ks[23], (L, D_MODEL), 0.02),
    }

def first_block(x, mem, ln0_g, ln0_b, w_in, w_a2, b_a, conv_w, conv_b, conv_ln_g, conv_ln_b,
              gla_norm_g, w_mix_out, ln1_g, ln1_b, w_xq, w_xkv, w_xo, ln2_g, ln2_b,
              w_ffn_in, w_ffn_out, ln3_g, ln3_b):
    h = layer_norm(x, ln0_g, ln0_b)
    for l in range(DEPTH):
        mix = hybrid_mixer(h, w_in[l], w_a2[l], b_a[l], conv_w[l], conv_b[l], conv_ln_g[l],
                           conv_ln_b[l], gla_norm_g[l], w_mix_out[l])
        h = layer_norm(DEEPNORM_ALPHA * h + mix, ln1_g[l], ln1_b[l])
        xa = memory_cross_attention(h, mem, w_xq[l], w_xkv[l], w_xo[l])
        h = layer_norm(DEEPNORM_ALPHA * h + xa, ln2_g[l], ln2_b[l])
        ff = swiglu(h, w_ffn_in[l], w_ffn_out[l])
        h = layer_norm(DEEPNORM_ALPHA * h + ff, ln3_g[l], ln3_b[l])
    return h


GRID_W = 64
CTX_LEN = 256
N_MIXERS = 2
N_MLA_LAYERS = (DEPTH + N_MIXERS - 1) // N_MIXERS
N_POOL_LAYERS = DEPTH // N_MIXERS
MLA_HEADS = 8
QK_NOPE_DIM = 128
QK_ROPE_DIM = 64
V_HEAD_DIM = 128
Q_LORA_RANK = 384
KV_LORA_RANK = 256
MLA_IN_DIM = Q_LORA_RANK + KV_LORA_RANK + QK_ROPE_DIM
ROPE_THETA = 10000.0
Q_BLOCK = 128
POOL_WINDOWS = (2, 4, 8, 16)
N_POOL_GROUPS = 4
POOL_GROUP_DIM = D_MODEL // N_POOL_GROUPS
PEER_HEADS = 8
PEER_N_KEYS = 128
PEER_N_EXPERTS = PEER_N_KEYS * PEER_N_KEYS
PEER_QUERY_DIM = 256
PEER_HALF = PEER_QUERY_DIM // 2
PEER_TOPK = 16
PEER_BLOCK = 128
RMS_EPS = 1e-6
DEEPNORM_ALPHA_2 = (2.0 * DEPTH) ** 0.25
DEEPNORM_BETA_2 = (8.0 * DEPTH) ** -0.25
N_MOD = 6


def _layernorm(x, g, b):
    xf = x.astype(jnp.float32)
    mu = jnp.mean(xf, axis=-1, keepdims=True)
    var = jnp.mean(jnp.square(xf - mu), axis=-1, keepdims=True)
    return ((xf - mu) * lax.rsqrt(var + LN_EPS) * g + b).astype(x.dtype)

def _rmsnorm(x, g):
    xf = x.astype(jnp.float32)
    return (xf * lax.rsqrt(jnp.mean(jnp.square(xf), axis=-1, keepdims=True) + RMS_EPS) * g).astype(x.dtype)

def _axial_rope_tables(n_tokens):
    rows_n = n_tokens // GRID_W
    row = jnp.repeat(jnp.arange(rows_n), GRID_W).astype(jnp.float32)
    col = jnp.tile(jnp.arange(GRID_W), rows_n).astype(jnp.float32)
    n_freq = QK_ROPE_DIM // 4
    freqs = ROPE_THETA ** (-jnp.arange(n_freq, dtype=jnp.float32) / n_freq)
    ang = jnp.concatenate([row[:, None] * freqs, col[:, None] * freqs], axis=-1)
    return jnp.cos(ang), jnp.sin(ang)

def _apply_rope(x, cos, sin):
    half = x.shape[-1] // 2
    xf = x.astype(jnp.float32)
    x1, x2 = xf[..., :half], xf[..., half:]
    return jnp.concatenate([x1 * cos - x2 * sin, x1 * sin + x2 * cos], axis=-1).astype(x.dtype)

def _block_attention(q, k, v):
    b, s, h, dk = q.shape
    scale = dk ** -0.5
    qb = q.reshape(b, s // Q_BLOCK, Q_BLOCK, h, dk).transpose(1, 0, 2, 3, 4)

    def one(qblk):
        sc = jnp.einsum('bqhd,bkhd->bhqk', qblk, k, preferred_element_type=jnp.float32) * scale
        p = jax.nn.softmax(sc, axis=-1).astype(v.dtype)
        return jnp.einsum('bhqk,bkhd->bqhd', p, v)

    o = lax.map(one, qb)
    return o.transpose(1, 0, 2, 3, 4).reshape(b, s, h * v.shape[-1])

def _mla_qkv(h, rope, w_in, q_norm_g, kv_norm_g, w_uq, w_ukv, with_queries):
    b, l, _ = h.shape
    z = h @ w_in
    c_q = z[..., :Q_LORA_RANK]
    c_kv = z[..., Q_LORA_RANK:Q_LORA_RANK + KV_LORA_RANK]
    k_rope = z[..., Q_LORA_RANK + KV_LORA_RANK:]
    kv = (_rmsnorm(c_kv, kv_norm_g) @ w_ukv).reshape(b, l, MLA_HEADS, QK_NOPE_DIM + V_HEAD_DIM)
    k_nope, v = kv[..., :QK_NOPE_DIM], kv[..., QK_NOPE_DIM:]
    if rope is not None:
        cos, sin = rope
        k_rope = _apply_rope(k_rope, cos, sin)
    k = jnp.concatenate([k_nope, jnp.broadcast_to(k_rope[:, :, None, :], (b, l, MLA_HEADS, QK_ROPE_DIM))], axis=-1)
    if not with_queries:
        return None, k, v
    q = (_rmsnorm(c_q, q_norm_g) @ w_uq).reshape(b, l, MLA_HEADS, QK_NOPE_DIM + QK_ROPE_DIM)
    q_nope, q_rope = q[..., :QK_NOPE_DIM], q[..., QK_NOPE_DIM:]
    if rope is not None:
        q_rope = _apply_rope(q_rope, cos[:, None, :], sin[:, None, :])
    return jnp.concatenate([q_nope, q_rope], axis=-1), k, v

def _centred_mean_minus_self(x, window):
    b, l, ch = x.shape
    xf = x.astype(jnp.float32)
    cs = jnp.concatenate([jnp.zeros((b, 1, ch), jnp.float32), jnp.cumsum(xf, axis=1)], axis=1)
    t = jnp.arange(l)
    lo = jnp.clip(t - window // 2, 0, l)
    hi = jnp.clip(t + window // 2, 0, l)
    tot = jnp.take(cs, hi, axis=1) - jnp.take(cs, lo, axis=1)
    cnt = (hi - lo).astype(jnp.float32)[None, :, None]
    return (tot / cnt - xf).astype(x.dtype)

def _pool_mixer(h, w_in, w_grp, scale, w_out):
    b, l, _ = h.shape
    zg = (h @ w_in).reshape(b, l, N_POOL_GROUPS, POOL_GROUP_DIM)
    pooled = jnp.stack([_centred_mean_minus_self(zg[:, :, g], POOL_WINDOWS[g]) for g in range(N_POOL_GROUPS)], axis=2)
    y = jnp.einsum('blgc,gcd->blgd', pooled, w_grp).reshape(b, l, D_MODEL) * scale
    return y @ w_out

def _peer(h, w_q, k1, k2, u_tab, v_tab):
    b, l, d = h.shape
    q = (h @ w_q).reshape(b, l, PEER_HEADS, 2, PEER_HALF)
    s1 = jnp.einsum('blhc,hnc->blhn', q[..., 0, :], k1, preferred_element_type=jnp.float32)
    s2 = jnp.einsum('blhc,hnc->blhn', q[..., 1, :], k2, preferred_element_type=jnp.float32)
    v1, i1 = lax.top_k(s1, PEER_TOPK)
    v2, i2 = lax.top_k(s2, PEER_TOPK)
    cand_s = (v1[..., :, None] + v2[..., None, :]).reshape(b, l, PEER_HEADS, PEER_TOPK * PEER_TOPK)
    cand_i = (i1[..., :, None] * PEER_N_KEYS + i2[..., None, :]).reshape(b, l, PEER_HEADS, PEER_TOPK * PEER_TOPK)
    top_s, pos = lax.top_k(cand_s, PEER_TOPK)
    idx = jnp.take_along_axis(cand_i, pos, axis=-1)
    g = jax.nn.softmax(top_s, axis=-1).astype(h.dtype)
    n_blk = (b * l) // PEER_BLOCK
    n_sel = PEER_HEADS * PEER_TOPK
    hb = h.reshape(n_blk, PEER_BLOCK, d)
    ib = idx.reshape(n_blk, PEER_BLOCK, n_sel)
    gb = g.reshape(n_blk, PEER_BLOCK, n_sel)

    def one(args):
        hx, ix, gx = args
        u = jnp.take(u_tab, ix, axis=0)
        a = jax.nn.gelu(jnp.einsum('ted,td->te', u, hx), approximate=False)
        vv = jnp.take(v_tab, ix, axis=0)
        return jnp.einsum('te,ted->td', gx * a, vv)

    return lax.map(one, (hb, ib, gb)).reshape(b, l, d)

def _post_norm(x, y, gate, g, b):
    return _layernorm(DEEPNORM_ALPHA_2 * x + gate * y, g, b)

def second_inputs(seed: int = 0) -> dict:
    key = jax.random.key(seed)
    ks = jax.random.split(key, 24)
    nrm = lambda k, shp, s: jax.random.normal(k, shp, jnp.float32) * s
    D = D_MODEL
    return {
        "x": nrm(ks[0], (BATCH, SEQ, D), 1.0),
        "c": nrm(ks[1], (BATCH, D), 1.0),
        "ctx": nrm(ks[2], (BATCH, CTX_LEN, D), 1.0),
        "c_ctx": nrm(ks[3], (D,), 1.0),
        "w_mod": nrm(ks[4], (DEPTH, D, N_MOD * D), 0.5 * D ** -0.5),
        "b_mod": nrm(ks[5], (DEPTH, N_MOD * D), 0.02),
        "ln_g": 1.0 + nrm(ks[6], (DEPTH, 2, D), 0.05),
        "ln_b": nrm(ks[7], (DEPTH, 2, D), 0.02),
        "mla_w_in": nrm(ks[8], (N_MLA_LAYERS, D, MLA_IN_DIM), D ** -0.5),
        "mla_q_norm": 1.0 + nrm(ks[9], (N_MLA_LAYERS, Q_LORA_RANK), 0.05),
        "mla_kv_norm": 1.0 + nrm(ks[10], (N_MLA_LAYERS, KV_LORA_RANK), 0.05),
        "mla_w_uq": nrm(ks[11], (N_MLA_LAYERS, Q_LORA_RANK, MLA_HEADS * (QK_NOPE_DIM + QK_ROPE_DIM)), Q_LORA_RANK ** -0.5),
        "mla_w_ukv": nrm(ks[12], (N_MLA_LAYERS, KV_LORA_RANK, MLA_HEADS * (QK_NOPE_DIM + V_HEAD_DIM)), KV_LORA_RANK ** -0.5),
        "mla_w_o": nrm(ks[13], (N_MLA_LAYERS, MLA_HEADS * V_HEAD_DIM, D), DEEPNORM_BETA_2 * (MLA_HEADS * V_HEAD_DIM) ** -0.5),
        "pool_w_in": nrm(ks[14], (N_POOL_LAYERS, D, D), D ** -0.5),
        "pool_w_grp": nrm(ks[15], (N_POOL_LAYERS, N_POOL_GROUPS, POOL_GROUP_DIM, POOL_GROUP_DIM), POOL_GROUP_DIM ** -0.5),
        "pool_scale": 1.0 + nrm(ks[16], (N_POOL_LAYERS, D), 0.1),
        "pool_w_out": nrm(ks[17], (N_POOL_LAYERS, D, D), DEEPNORM_BETA_2 * D ** -0.5),
        "peer_w_q": nrm(ks[18], (DEPTH, D, PEER_HEADS * PEER_QUERY_DIM), D ** -0.5),
        "peer_k1": nrm(ks[19], (DEPTH, PEER_HEADS, PEER_N_KEYS, PEER_HALF), PEER_HALF ** -0.5),
        "peer_k2": nrm(ks[20], (DEPTH, PEER_HEADS, PEER_N_KEYS, PEER_HALF), PEER_HALF ** -0.5),
        "peer_u": nrm(ks[21], (DEPTH, PEER_N_EXPERTS, D), D ** -0.5),
        "peer_v": nrm(ks[22], (DEPTH, PEER_N_EXPERTS, D), DEEPNORM_BETA_2),
    }

def second_block(x, c, ctx, c_ctx, w_mod, b_mod, ln_g, ln_b, mla_w_in, mla_q_norm, mla_kv_norm, mla_w_uq, mla_w_ukv, mla_w_o,
              pool_w_in, pool_w_grp, pool_scale, pool_w_out, peer_w_q, peer_k1, peer_k2, peer_u, peer_v):
    b, s, _ = x.shape
    rope = _axial_rope_tables(s)
    silu_c = jax.nn.silu(c)
    silu_ctx = jax.nn.silu(c_ctx)
    for i in range(DEPTH):
        mixer = i % N_MIXERS
        j = i // N_MIXERS
        ctx_needed = any(k % N_MIXERS == 0 for k in range(i + 1, DEPTH))
        ml = (silu_c @ w_mod[i] + b_mod[i])[:, None, :]
        mc = silu_ctx @ w_mod[i] + b_mod[i]
        sh1, sc1, g1, sh2, sc2, g2 = jnp.split(ml, N_MOD, axis=-1)
        csh1, csc1, cg1, csh2, csc2, cg2 = jnp.split(mc, N_MOD, axis=-1)
        hx = x * (1.0 + sc1) + sh1
        hc = ctx * (1.0 + csc1) + csh1
        if mixer == 0:
            w = (mla_w_in[j], mla_q_norm[j], mla_kv_norm[j], mla_w_uq[j], mla_w_ukv[j])
            q, k, v = _mla_qkv(hx, rope, *w, True)
            qc, kc, vc = _mla_qkv(hc, None, *w, ctx_needed)
            y = _block_attention(q, jnp.concatenate([k, kc], axis=1), jnp.concatenate([v, vc], axis=1)) @ mla_w_o[j]
            if ctx_needed:
                yc = _block_attention(qc, kc, vc) @ mla_w_o[j]
        else:
            w = (pool_w_in[j], pool_w_grp[j], pool_scale[j], pool_w_out[j])
            y = _pool_mixer(hx, *w)
            if ctx_needed:
                yc = _pool_mixer(hc, *w)
        pw = (peer_w_q[i], peer_k1[i], peer_k2[i], peer_u[i], peer_v[i])
        x = _post_norm(x, y, g1, ln_g[i, 0], ln_b[i, 0])
        x = _post_norm(x, _peer(x * (1.0 + sc2) + sh2, *pw), g2, ln_g[i, 1], ln_b[i, 1])
        if ctx_needed:
            ctx = _post_norm(ctx, yc, cg1, ln_g[i, 0], ln_b[i, 0])
            ctx = _post_norm(ctx, _peer(ctx * (1.0 + csc2) + csh2, *pw), cg2, ln_g[i, 1], ln_b[i, 1])
    return x


def setup_inputs(seed=0):
    out = dict(first_inputs(seed))
    for name, value in second_inputs(seed + 1).items():
        if name != "x":
            out[name + "_2"] = value
    return out


def reference(
    x, mem, ln0_g, ln0_b, w_in, w_a2, b_a, conv_w, conv_b, conv_ln_g, conv_ln_b, gla_norm_g,
    w_mix_out, ln1_g, ln1_b, w_xq, w_xkv, w_xo, ln2_g, ln2_b, w_ffn_in, w_ffn_out, ln3_g, ln3_b,
    c_2, ctx_2, c_ctx_2, w_mod_2, b_mod_2, ln_g_2, ln_b_2, mla_w_in_2, mla_q_norm_2,
    mla_kv_norm_2, mla_w_uq_2, mla_w_ukv_2, mla_w_o_2, pool_w_in_2, pool_w_grp_2, pool_scale_2,
    pool_w_out_2, peer_w_q_2, peer_k1_2, peer_k2_2, peer_u_2, peer_v_2,
):
    x = first_block(
        x, mem, ln0_g, ln0_b, w_in, w_a2, b_a, conv_w, conv_b, conv_ln_g, conv_ln_b, gla_norm_g,
        w_mix_out, ln1_g, ln1_b, w_xq, w_xkv, w_xo, ln2_g, ln2_b, w_ffn_in, w_ffn_out, ln3_g,
        ln3_b,
    )
    return second_block(
        x, c_2, ctx_2, c_ctx_2, w_mod_2, b_mod_2, ln_g_2, ln_b_2, mla_w_in_2, mla_q_norm_2,
        mla_kv_norm_2, mla_w_uq_2, mla_w_ukv_2, mla_w_o_2, pool_w_in_2, pool_w_grp_2,
        pool_scale_2, pool_w_out_2, peer_w_q_2, peer_k1_2, peer_k2_2, peer_u_2, peer_v_2,
    )


_drawn_inputs = setup_inputs


def setup_inputs(seed=0):
    import zlib

    import numpy as np

    out = dict(_drawn_inputs(seed))
    spreads = {}
    factors = {'b_a': 8.0,
     'conv_b': 4.563,
     'conv_ln_g': 6.587,
     'conv_ln_b': 7.6,
     'gla_norm_g': 7.462,
     'ctx_2': 6.357,
     'c_ctx_2': 3.205,
     'b_mod_2': 3.349,
     'mla_q_norm_2': 8.0,
     'mla_kv_norm_2': 8.0,
     'mla_w_uq_2': 4.354,
     'pool_scale_2': 4.647}
    for name, (base, spread) in spreads.items():
        noise = np.random.default_rng([zlib.crc32(name.encode()), seed]).standard_normal(out[name].shape)
        drawn = base * np.exp(spread * noise) if base else spread * noise
        out[name] = __import__('jax').numpy.asarray(drawn.astype(out[name].dtype))
    for name, factor in factors.items():
        out[name] = (out[name] * factor).astype(out[name].dtype)
    return out
```

```python
from contextlib import ExitStack

import numpy as np

import concourse.bass as bass
from concourse import mybir

F32 = mybir.dt.float32
U32 = mybir.dt.uint32
ALU = mybir.AluOpType
ACT = mybir.ActivationFunctionType
AX_X = mybir.AxisListType.X

P = 128
D = 1024
KD = D // P
T = 256
TT = T // P
DEPTH = 2
ALPHA = (2 * DEPTH) ** 0.25
LN_EPS, RMS_EPS = 1e-5, 1e-6

CONV, TAPS = 512, 31
CF = CONV // P
GH, GK, GV, CHUNK = 4, 64, 128, 64
GF = GH * GK // P
NCHUNK = T // CHUNK
RANK = 16
XH = 4
FF = 2816
KF = FF // P

MH, NOPE, ROPE, VD = 8, 128, 64, 128
QL, KVL = 384, 256
GROUPS, WINDOWS = 4, (2, 4, 8, 16)
PH, NK, TOPK = 8, 128, 16
NEXP = NK * NK

PANEL = KD * 4 * P
SLOTS = 4
NBANK = 4
NEG = -3.0e38


def layer_panels():
    mod = iter([("mod", i) for i in range(12)])
    take = lambda n: [next(mod) for _ in range(n)]
    return ([("glu", 0), ("glu", 1), ("qk", 0), ("v", 0), ("r", 0), ("xk", 0), ("xk", 1), ("xv", 0), ("xv", 1)]
            + [("mix", 0), ("mix", 1)] + take(3) + [("xq", 0), ("xq", 1)] + take(3)
            + [("xo", 0), ("xo", 1)] + take(3) + [("fi", i) for i in range(11)]
            + [("fo", i) for i in range(8)] + take(3))


A_PANELS = layer_panels()
B_PANELS = ([("zi", 0), ("zi", 1), ("uq", 0), ("uq", 1), ("ukv", 0), ("wo", 0), ("wo", 1)]
            + [("pq", i) for i in range(4)] + [("pk", 0)])
C_PANELS = ([("pin", 0), ("pin", 1), ("grp", 0), ("pout", 0), ("pout", 1)]
            + [("pq", i) for i in range(4)] + [("pk", 0)])
NPANELS = DEPTH * len(A_PANELS) + len(B_PANELS) + len(C_PANELS)

A_TILES = ([("glu", i) for i in range(8)] + [("qk", i) for i in range(4)] + [("v", i) for i in range(2)]
           + [("r", i) for i in range(4)] + [("xk", i) for i in range(8)] + [("upd", i) for i in range(3)]
           + [("xv", i) for i in range(4)] + [("o", i) for i in range(4)]
           + [("mix", i) for i in range(8)] + [("xq", i) for i in range(8)] + [("sc", i) for i in range(8)]
           + [("pt", i) for i in range(4)] + [("ox", i) for i in range(8)] + [("xo", i) for i in range(8)]
           + [("fi", i) for i in range(44)] + [("fo", i) for i in range(8)])
PEER_TILES = ([("pq", i) for i in range(8)] + [("ht", i) for i in range(4)] + [("pq", i) for i in range(8, 16)]
              + [("ps", i) for i in range(8)])
B_TILES = ([("zi", i) for i in range(7)] + [("uq", i) for i in range(12)] + [("kn", i) for i in range(8)]
           + [("vm", i) for i in range(8)]
           + [t for h in range(MH) for t in [("sc", 2 * h), ("sc", 2 * h + 1)]
              + ([("pt", 2 * h - 2), ("pt", 2 * h - 1), ("ox", h - 1)] if h else [])]
           + [("pt", 14), ("pt", 15), ("ox", 7)] + [("wo", i) for i in range(8)] + PEER_TILES)
C_TILES = ([("pin", i) for i in range(8)] + [("grp", i) for i in range(8)] + [("pout", i) for i in range(8)]
           + PEER_TILES)


LAST_TILE = {("v", 0): ("v", 1), ("xv", 0): ("xv", 1), ("xv", 1): ("xv", 3), ("zi", 1): ("zi", 6), ("uq", 0): ("uq", 5),
             ("uq", 1): ("uq", 11), ("ukv", 0): ("vm", 7), ("grp", 0): ("grp", 7), ("pk", 0): ("ps", 7),
             **{("fo", i): ("fo", i) for i in range(8)}}


def columns(widths):
    at, out = 0, {}
    for name, w in widths:
        out[name] = slice(at, at + w)
        at += w
    return out, at


VEC_A, NVEC_A = columns([("ln1_g", 8), ("ln1_b", 8), ("ln2_g", 8), ("ln2_b", 8), ("ln3_g", 8), ("ln3_b", 8),
                         ("conv_w", CF * TAPS), ("conv_b", CF), ("cln_g", CF), ("cln_b", CF), ("gla_g", 1),
                         ("b_a", GF), ("w_low", KD * RANK), ("w_a2", GH * GK), ("b_mod", 48)])
VEC_B, NVEC_B = columns([("ln0_g", 8), ("ln0_b", 8), ("c", 16), ("ln_g", 32), ("ln_b", 32),
                         ("q_norm", 3), ("kv_norm", 2), ("pool_scale", 8)])
CONST, NCONST = columns([("ident", P), ("cos", 2 * T), ("sin", 2 * T), ("scan", T), ("iota", TOPK),
                         ("invcnt", GROUPS * T)])

ARENA = 28928
LN_W = [("xc", KD * T), ("sq", KD * T), ("sd", T), ("rstd", T)]
A_MEM, A_END = columns(LN_W + [
    ("xk", KD * T), ("xv", TT * D), ("mix", KD * T),
    ("glu", CF * (TAPS - 1 + T)), ("sig", 4 * T), ("cy", CF * T), ("q", GF * T), ("k", GF * T), ("r", CF * T),
    ("v", TT * GH * GV), ("low", T), ("z", GF * T), ("za", GF * T), ("bc", GF * T), ("ep", GF * T),
    ("en", GF * T), ("ed", GF * T), ("qe", GF * T), ("ke", GF * T), ("kd", GF * T),
    ("kdt", TT * GH * GK), ("att", 8 * P), ("st", 3 * GF * GV), ("o", GH * T), ("rs", GH * T)])
A_SHARE = A_MEM["glu"].start
X_MEM, X_END = columns([("pad", A_SHARE), ("qx", KD * T), ("p", 8 * T), ("pt", XH * TT * T), ("ox", KD * T)])
F_MEM, F_END = columns([("pad", A_SHARE), ("sg", 4 * T), ("hid", KF * T)])
B_MEM, B_END = columns(LN_W + [
    ("h", KD * 2 * T), ("cq", 3 * T), ("ckv", 2 * 2 * T), ("kr", 2 * 2 * T), ("kro", 2 * 2 * T),
    ("qr", 4 * T), ("qro", 4 * T), ("qn", MH * T), ("kn", MH * 2 * T), ("vm", 4 * D), ("tmp", 2 * 2 * T),
    ("p", 2 * 2 * T), ("pt", 2 * 4 * P)])
B_OX = B_MEM["h"].start
C_MEM, C_END = columns(LN_W + [("zp", KD * (T + 16)), ("s1", 2 * (T + 16)), ("s2", 2 * (T + 16)),
                               ("pooled", KD * T), ("yg", KD * T)])
RING = 8
P_MEM, P_END = columns([
    ("ring", RING * 2 * D), ("s12", TT * 2 * PH * NK), ("hc", D), ("sc", 2 * PH * NK),
    ("wk", 2 * NK), ("v16", 2 * TOPK), ("i16", 2 * TOPK), ("if", 2 * TOPK), ("cand", T), ("cw", T), ("top", TOPK),
    ("pos", TOPK), ("ab", 2 * TOPK), ("abf", 2 * TOPK), ("oh", T), ("sel", 2 * TOPK), ("idf", TOPK),
    ("idx", PH * TOPK), ("g", PH * TOPK), ("gs", 4), ("dot", PH * TOPK), ("act", PH * TOPK), ("cf", PH * TOPK),
    ("acc", 2 * D)])
Q_MEM, _ = columns([("pad", P_MEM["hc"].start), ("hp", KD * T), ("pq", 16 * T)])
assert max(A_END, X_END, F_END, B_END, C_END, P_END, _) <= ARENA, (A_END, X_END, F_END, B_END, C_END, P_END, _)


class Ring:

    def __init__(self, tiles):
        self.order = {t: n for n, t in enumerate(tiles)}
        assert len(self.order) == len(tiles)

    def at(self, stage, i):
        n = self.order[(stage, i)]
        return n % NBANK, n // NBANK


def build_program(nc, panels, vec_a, vec_b, consts, mask_in, acts, tables, out):
    with ExitStack() as ctx:
        def sb(name, cols, dt=F32):
            return ctx.enter_context(nc.sbuf_tensor(name, [P, cols], dt))

        sems = {}

        def sem(name):
            if name not in sems:
                sems[name] = ctx.enter_context(nc.semaphore(name))
            return sems[name]

        ring = sb("weight_ring", SLOTS * PANEL)
        xT = sb("xT", KD * T)
        memT = sb("memT", KD * T)
        ones = sb("ones", P)
        cst = sb("cst", NCONST)
        mask = sb("causal_mask", P, U32)
        va = sb("va", NVEC_A)
        vb = sb("vb", NVEC_B)
        eps = sb("eps", 2)
        silu_c = sb("silu_c", 2 * KD)
        modT = sb("modT", DEPTH * 96)
        arena = sb("arena", ARENA)
        T_ = [ctx.enter_context(nc.psum_tensor(f"tile{b}", [P, 512], F32)) for b in range(NBANK)]
        M = [ctx.enter_context(nc.psum_tensor(f"misc{b}", [P, 512], F32)) for b in range(4)]

        def cut(mem, name, pat=None, **kw):
            ap = arena[:, mem[name]]
            return ap.rearrange(pat, **kw) if pat else ap

        x3 = xT[:, :].rearrange("p (f t) -> p f t", f=KD)
        mem3 = memT[:, :].rearrange("p (f t) -> p f t", f=KD)
        sc3 = silu_c[:, :].rearrange("p (f c) -> p f c", c=2)
        ident = cst[:, CONST["ident"]]
        mod4 = modT[:, :].rearrange("p (l j c) -> p l j c", l=DEPTH, c=2)
        xc = cut(A_MEM, "xc", "p (f t) -> p f t", f=KD)
        sq = cut(A_MEM, "sq", "p (f t) -> p f t", f=KD)
        sd, rstd = cut(A_MEM, "sd"), cut(A_MEM, "rstd")

        def vcol(tensor, table, name, i=0):
            c = table[name].start + i
            return tensor[:, c:c + 1]

        class PE:

            def __init__(self, pe, panel_list, tiles):
                self.pe, self.list, self.n, self.tiles = pe, panel_list, 0, Ring(tiles)

            def panel(self, stage, i):
                assert self.list[self.n] == (stage, i), (self.list[self.n], stage, i)
                n, self.n = self.n, self.n + 1
                if n >= SLOTS:
                    self.pe.wait_ge(sem(f"panel_landed{n % SLOTS}"), 16 * (n // SLOTS))
                return ring[:, (n % SLOTS) * PANEL:(n % SLOTS + 1) * PANEL]

            def bank(self, stage, i):
                b, use = self.tiles.at(stage, i)
                if use:
                    self.pe.wait_ge(sem(f"bank_read{b}"), use)
                return T_[b]

            def filled(self, ins, stage, i):
                ins.then_inc(sem(f"bank_filled{self.tiles.at(stage, i)[0]}"), 1)

            def feature_tiles(self, w, stage, first, count, K, rhs, N):
                for j in range(count):
                    bank = self.bank(stage, first + j)
                    for k in range(K):
                        c = (j * K + k) * P
                        ins = nc.tensor.matmul(bank[:, 0:N], w[:, c:c + P], rhs[:, k, 0:N],
                                               start=(k == 0), stop=(k == K - 1))
                    self.filled(ins, stage, first + j)

            def token_tiles(self, w, stage, first, count, K, lhs, width=512, off=0):
                for j in range(count):
                    bank = self.bank(stage, first + j)
                    for k in range(K):
                        ins = nc.tensor.matmul(bank[:, :], lhs[:, k, j * P:(j + 1) * P],
                                               w[:, off + k * width:off + k * width + 512],
                                               start=(k == 0), stop=(k == K - 1))
                    self.filled(ins, stage, first + j)

        def stat_pe(wait_written, signal, src, n, bank):
            for f in range(n):
                wait_written(f)
                ins = nc.tensor.matmul(bank, ones[:, :], src[:, f, :], start=(f == 0), stop=(f == n - 1))
            ins.then_inc(sem(signal), 1)

        def norm_pe(pe, ln, wait_written, src, n):
            stat_pe(wait_written, f"{ln}_sum", src, n, M[0][:, 0:T])
            stat_pe(lambda f: pe.wait_ge(sem(f"{ln}_sq"), f + 1), f"{ln}_var", sq, n, M[3][:, T:2 * T])

        def norm_dve(dve, ln, src, n):
            dve.wait_ge(sem(f"{ln}_sum"), 1)
            for f in range(n):
                nc.vector.scalar_tensor_tensor(out=xc[:, f, :], in0=M[0][:, 0:T], scalar=-1.0 / (n * P),
                                               in1=src[:, f, :], op0=ALU.mult, op1=ALU.add
                                               ).then_inc(sem(f"{ln}_centred"), 1)
            dve.wait_ge(sem(f"{ln}_sd"), 1)
            nc.vector.reciprocal(rstd, sd).then_inc(sem(f"{ln}_rstd"), 1)
            dve.wait_ge(sem(f"{ln}_rstd"), 1)
            dve.wait_ge(sem(f"{ln}_centred"), n)
            for f in range(n):
                nc.vector.tensor_tensor(xc[:, f, :], xc[:, f, :], rstd, ALU.mult
                                        ).then_inc(sem(f"{ln}_scaled"), 1)

        def norm_act(act, ln, n, dst, tensor, table, g, b, off=0, func=ACT.Identity):
            for f in range(n):
                act.wait_ge(sem(f"{ln}_centred"), f + 1)
                nc.scalar.activation(sq[:, f, :], xc[:, f, :], ACT.Square).then_inc(sem(f"{ln}_sq"), 1)
            act.wait_ge(sem(f"{ln}_var"), 1)
            nc.scalar.activation(sd, M[3][:, T:2 * T], ACT.Sqrt, scale=1.0 / (n * P), bias=eps[:, 0:1]
                                 ).then_inc(sem(f"{ln}_sd"), 1)
            for f in range(n):
                act.wait_ge(sem(f"{ln}_scaled"), f + 1)
                nc.scalar.activation(dst[:, f, :], xc[:, f, :], func, scale=vcol(tensor, table, g, off + f),
                                     bias=vcol(tensor, table, b, off + f)).then_inc(sem(f"{ln}_out"), 1)

        class Reader:

            def __init__(self, eng, tiles):
                self.eng, self.tiles = eng, Ring(tiles)

            def full(self, stage, i):
                b, use = self.tiles.at(stage, i)
                self.eng.wait_ge(sem(f"bank_filled{b}"), use + 1)
                return T_[b]

            def free(self, ins, stage, i):
                ins.then_inc(sem(f"bank_read{self.tiles.at(stage, i)[0]}"), 1)

            def read_wait(self, stage, i):
                b, use = self.tiles.at(stage, i)
                self.eng.wait_ge(sem(f"bank_read{b}"), use + 1)

        def stream(sp, panel_list, tiles, base, following):
            rd, n = Reader(sp, tiles), len(panel_list)

            def wait_used(stage, i):
                if stage == "mod":
                    sp.wait_ge(sem("mod_filled"), i + 1)
                else:
                    rd.full(*LAST_TILE.get((stage, i), (stage, 4 * i + 3)))

            def load(j, slot, landed):
                sp.dma_start(ring[:, slot * PANEL:(slot + 1) * PANEL],
                             panels[bass.ds(base + j, 1)].rearrange("a p c -> (a p) c")).then_inc(sem(landed), 16)

            for j in range(SLOTS, n):
                wait_used(*panel_list[j - SLOTS])
                load(j, j % SLOTS, f"panel_landed{j % SLOTS}")
            if following:
                for j in range(SLOTS):
                    wait_used(*panel_list[max(i for i in range(n) if i % SLOTS == j)])
                    load(n + j, j, "next_landed")
                sp.wait_ge(sem("next_landed"), 16 * SLOTS)

        def clear_semaphores():
            with nc.Block() as block:
                @block.sync
                def _(sp):
                    for name, s in sems.items():
                        if not name.startswith("row_landed"):
                            sp.sem_clear(s)

        with nc.Block() as block:
            @block.sync
            def _(sp):
                sp.dma_start(xT[:, :], acts[0]).then_inc(sem("x_landed"), 16)
                sp.dma_start(vb[:, :], vec_b).then_inc(sem("vec_landed"), 16)
                sp.dma_start(cst[:, :], consts).then_inc(sem("const_landed"), 16)
                sp.dma_start(mask[:, :], mask_in).then_inc(sem("const_landed"), 16)
                sp.dma_start(memT[:, :], acts[1]).then_inc(sem("const_landed"), 16)
                for j in range(SLOTS):
                    sp.dma_start(ring[:, j * PANEL:(j + 1) * PANEL], panels[j]).then_inc(sem("next_landed"), 16)
                sp.wait_ge(sem("const_landed"), 48)
                sp.wait_ge(sem("next_landed"), 16 * SLOTS)

            @block.gpsimd
            def _(pool):
                nc.gpsimd.memset(ones[:, :], 1.0).then_inc(sem("ones_set"), 1)
                nc.gpsimd.memset(eps[:, 0:1], LN_EPS).then_inc(sem("eps_set"), 1)
                nc.gpsimd.memset(eps[:, 1:2], RMS_EPS).then_inc(sem("eps_set"), 1)

            @block.tensor
            def _(pe):
                pe.wait_ge(sem("ones_set"), 1)
                pe.wait_ge(sem("x_landed"), 16)
                for f in range(KD):
                    ins = nc.tensor.matmul(M[0][:, 0:T], ones[:, :], x3[:, f, :], start=(f == 0), stop=(f == KD - 1))
                ins.then_inc(sem("ln0_sum"), 1)
                stat_pe(lambda f: pe.wait_ge(sem("ln0_sq"), f + 1), "ln0_var", sq, KD, M[3][:, T:2 * T])

            @block.vector
            def _(dve):
                dve.wait_ge(sem("x_landed"), 16)
                norm_dve(dve, "ln0", x3, KD)

            @block.scalar
            def _(act):
                act.wait_ge(sem("vec_landed"), 16)
                act.wait_ge(sem("eps_set"), 2)
                nc.scalar.activation(silu_c[:, :], vb[:, VEC_B["c"]], ACT.Silu)
                norm_act(act, "ln0", KD, x3, vb, VEC_B, "ln0_g", "ln0_b")
        clear_semaphores()

        glu = cut(A_MEM, "glu", "p (f t) -> p f t", f=CF)
        sig = cut(A_MEM, "sig", "p (f t) -> p f t", f=4)
        cy = cut(A_MEM, "cy", "p (f t) -> p f t", f=CF)
        mix = cut(A_MEM, "mix", "p (f t) -> p f t", f=KD)
        gq, gk = (cut(A_MEM, n, "p (f t) -> p f t", f=GF) for n in ("q", "k"))
        r = cut(A_MEM, "r", "p (f t) -> p f t", f=CF)
        v = cut(A_MEM, "v", "p (a n) -> p a n", a=TT)
        low = cut(A_MEM, "low")
        flat = {n: cut(A_MEM, n) for n in ("z", "za", "bc", "ep", "en", "ed", "qe", "ke", "kd", "q", "k")}
        gf = {n: cut(A_MEM, n, "p (f t) -> p f t", f=GF) for n in ("z", "za", "bc", "ep", "en", "ed", "qe", "ke", "kd")}
        kdt = cut(A_MEM, "kdt", "p (a n) -> p a n", a=TT)
        att = cut(A_MEM, "att", "p (a n) -> p a n", a=8)
        st = cut(A_MEM, "st", "p (c f n) -> p c f n", c=3, f=GF)
        o = cut(A_MEM, "o", "p (h t) -> p h t", h=GH)
        rs = cut(A_MEM, "rs", "p (h t) -> p h t", h=GH)
        xk = cut(A_MEM, "xk", "p (f t) -> p f t", f=KD)
        xv = cut(A_MEM, "xv", "p (a n) -> p a n", a=TT)
        qx = cut(X_MEM, "qx", "p (f t) -> p f t", f=KD)
        px = cut(X_MEM, "p", "p (a t) -> p a t", a=8)
        ptx = cut(X_MEM, "pt", "p (h m t) -> p h m t", h=XH, m=TT)
        oxx = cut(X_MEM, "ox", "p (f t) -> p f t", f=KD)
        sg = cut(F_MEM, "sg", "p (f t) -> p f t", f=4)
        hid = cut(F_MEM, "hid", "p (f t) -> p f t", f=KF)
        small = sb("small", 96)
        nmax, rsum, rinv = small[:, 0:16], small[:, 16:32], small[:, 32:48]
        conv_w = va[:, VEC_A["conv_w"]].rearrange("p (f j) -> p f j", f=CF)
        w_low = va[:, VEC_A["w_low"]].rearrange("p (k n) -> p k n", k=KD)
        w_a2 = va[0:RANK, VEC_A["w_a2"]]

        with nc.Fori(0, DEPTH) as layer:
            with nc.Block() as block:
                @block.sync
                def _(sp):
                    sp.dma_start(va[:, :], vec_a[bass.ds(layer, 1)].rearrange("a p c -> (a p) c")
                                 ).then_inc(sem("vec_landed"), 16)
                    stream(sp, A_PANELS, A_TILES, layer * len(A_PANELS), True)

                @block.tensor
                def _(pe):
                    e = PE(pe, A_PANELS, A_TILES)
                    rd = Reader(pe, A_TILES)

                    def full_panel(stage, i, rhs, count=4, K=KD):
                        e.feature_tiles(e.panel(stage, i), stage, 4 * i, count, K, rhs, T)

                    def mod_panel(i):
                        w = e.panel("mod", i)
                        for j in range(4):
                            c = 2 * (4 * i + j)
                            for k in range(KD):
                                ins = nc.tensor.matmul(M[3][:, c:c + 2], w[:, (j * KD + k) * P:(j * KD + k + 1) * P],
                                                       sc3[:, k, :], start=(k == 0), stop=(k == KD - 1))
                        ins.then_inc(sem("mod_filled"), 1)

                    full_panel("glu", 0, x3)
                    full_panel("glu", 1, x3)
                    pe.wait_ge(sem("vec_landed"), 16)
                    for k in range(KD):
                        ins = nc.tensor.matmul(M[0][0:RANK, 0:T], w_low[:, k, :], x3[:, k, :],
                                               start=(k == 0), stop=(k == KD - 1))
                    ins.then_inc(sem("low_filled"), 1)
                    full_panel("qk", 0, x3)
                    pe.wait_ge(sem("low_read"), 1)
                    for f in range(GF):
                        ins = nc.tensor.matmul(M[1][:, f * T:(f + 1) * T], w_a2[:, f * P:(f + 1) * P],
                                               low[0:RANK, :], start=True, stop=True)
                    ins.then_inc(sem("z_filled"), 1)
                    e.token_tiles(e.panel("v", 0), "v", 0, TT, KD, x3)
                    full_panel("r", 0, x3)
                    full_panel("xk", 0, mem3)
                    pe.wait_ge(sem("kd_made"), 1)
                    for a in range(TT):
                        for f in range(GF):
                            c = (a * GF + f) * P
                            ins = nc.tensor.transpose(M[2][:, c:c + P], gf["kd"][:, f, a * P:(a + 1) * P], ident)
                    ins.then_inc(sem("kdt_filled"), 1)
                    pe.wait_ge(sem("qe_made"), 2)
                    for h in (0, 2, 1, 3):
                        rows = slice((h % 2) * GK, (h % 2 + 1) * GK)
                        for a in range(TT):
                            n = (h // 2) * TT + a
                            ins = nc.tensor.matmul(M[h % 2][:, n * P:(n + 1) * P],
                                                   gf["ke"][rows, h // 2, a * P:(a + 1) * P],
                                                   gf["qe"][rows, h // 2, a * P:(a + 1) * P], start=True, stop=True)
                        if h >= 2:
                            ins.then_inc(sem("att_filled"), 1)
                    full_panel("xk", 1, mem3)
                    pe.wait_ge(sem("kdt_read"), 1)
                    rd.read_wait("v", 0)
                    rd.read_wait("v", 1)
                    for c in range(NCHUNK - 1):
                        bank = e.bank("upd", c)
                        rows = slice((c % 2) * CHUNK, (c % 2 + 1) * CHUNK)
                        for h in range(GH):
                            cols = slice((h // 2) * GV, (h // 2 + 1) * GV)
                            ins = nc.tensor.matmul(bank[(h % 2) * GK:(h % 2 + 1) * GK, cols],
                                                   kdt[rows, c // 2, h * GK:(h + 1) * GK],
                                                   v[rows, c // 2, h * GV:(h + 1) * GV], start=True, stop=True)
                        e.filled(ins, "upd", c)
                    for i in range(2):
                        e.token_tiles(e.panel("xv", i), "xv", 2 * i, TT, KD, mem3)
                    pe.wait_ge(sem("att_masked"), 8)
                    for c in range(NCHUNK - 1):
                        rd.read_wait("upd", c)
                    pe.wait_ge(sem("state_half"), 2)
                    for h in range(GH):
                        bank = e.bank("o", h)
                        rows = slice((h % 2) * GK, (h % 2 + 1) * GK)
                        for a in range(TT):
                            nc.tensor.matmul(bank[:, a * P:(a + 1) * P], v[:, a, h * GV:(h + 1) * GV],
                                             att[:, (h % 2) * 4 + (h // 2) * TT + a, :], start=True, stop=False)
                            for c in range(max(1, 2 * a), 2 * a + 2):
                                ins = nc.tensor.matmul(bank[:, c * CHUNK:(c + 1) * CHUNK],
                                                       st[rows, c - 1, h // 2, :],
                                                       gf["qe"][rows, h // 2, c * CHUNK:(c + 1) * CHUNK],
                                                       start=False, stop=(c == 2 * a + 1))
                        e.filled(ins, "o", h)
                    for h in range(GH):
                        pe.wait_ge(sem("osq_made"), h + 1)
                        nc.tensor.matmul(M[1 + h // 2][:, (h % 2) * T:(h % 2 + 1) * T], ones[:, :], sq[:, 4 + h, :],
                                         start=True, stop=True).then_inc(sem("rms_filled"), 1)
                    norm_pe(pe, "cln", lambda f: pe.wait_ge(sem("conv_made"), f + 1), cy, CF)
                    pe.wait_ge(sem("cln_out"), CF)
                    pe.wait_ge(sem("gated"), GH)
                    full_panel("mix", 0, mix)
                    full_panel("mix", 1, mix)
                    for i in range(0, 3):
                        mod_panel(i)
                    norm_pe(pe, "ln1", lambda f: rd.read_wait("mix", f), x3, KD)
                    pe.wait_ge(sem("ln1_out"), KD)
                    full_panel("xq", 0, x3)
                    full_panel("xq", 1, x3)
                    for h in range(XH):
                        for k in range(2):
                            rd.read_wait("xq", 2 * h + k)
                            rd.read_wait("xk", 2 * h + k)
                        for a in range(TT):
                            bank = e.bank("sc", h * TT + a)
                            for k in range(2):
                                ins = nc.tensor.matmul(bank[:, 0:T], qx[:, 2 * h + k, a * P:(a + 1) * P],
                                                       xk[:, 2 * h + k, :], start=(k == 0), stop=(k == 1))
                            e.filled(ins, "sc", h * TT + a)
                    for i in range(3, 6):
                        mod_panel(i)
                    for h in range(XH):
                        pe.wait_ge(sem("px_made"), TT * (h + 1))
                        bank = e.bank("pt", h)
                        for m in range(TT):
                            for a in range(TT):
                                ins = nc.tensor.transpose(bank[:, m * T + a * P:m * T + (a + 1) * P],
                                                          px[:, h * TT + a, m * P:(m + 1) * P], ident)
                        e.filled(ins, "pt", h)
                    for i in range(4):
                        rd.read_wait("xv", i)
                    for f in range(KD):
                        rd.read_wait("pt", f // 2)
                        bank = e.bank("ox", f)
                        for m in range(TT):
                            ins = nc.tensor.matmul(bank[:, 0:T], xv[:, m, f * P:(f + 1) * P], ptx[:, f // 2, m, :],
                                                   start=(m == 0), stop=(m == TT - 1))
                        e.filled(ins, "ox", f)
                    for f in range(KD):
                        rd.read_wait("ox", f)
                    full_panel("xo", 0, oxx)
                    full_panel("xo", 1, oxx)
                    for i in range(6, 9):
                        mod_panel(i)
                    norm_pe(pe, "ln2", lambda f: rd.read_wait("xo", f), x3, KD)
                    pe.wait_ge(sem("ln2_out"), KD)
                    for i in range(11):
                        full_panel("fi", i, x3)
                    for i in range(KD):
                        w = e.panel("fo", i)
                        bank = e.bank("fo", i)
                        for k in range(KF):
                            if i == 0:
                                rd.read_wait("fi", 2 * k + 1)
                            ins = nc.tensor.matmul(bank[:, 0:T], w[:, k * P:(k + 1) * P], hid[:, k, :],
                                                   start=(k == 0), stop=(k == KF - 1))
                        e.filled(ins, "fo", i)
                    for i in range(9, 12):
                        mod_panel(i)
                    norm_pe(pe, "ln3", lambda f: rd.read_wait("fo", f), x3, KD)

                @block.scalar
                def _(act):
                    rd = Reader(act, A_TILES)
                    for i in range(CF):
                        ins = nc.scalar.activation(sig[:, i, :], rd.full("glu", 2 * i)[:, 0:T], ACT.Sigmoid)
                        rd.free(ins, "glu", 2 * i)
                    act.wait_ge(sem("low_filled"), 1)
                    nc.scalar.activation(low[0:RANK, :], M[0][0:RANK, 0:T], ACT.Copy).then_inc(sem("low_read"), 1)
                    for i in range(4):
                        dst = (gq if i < GF else gk)[:, i % GF, :]
                        ins = nc.scalar.activation(dst, rd.full("qk", i)[:, 0:T], ACT.Copy,
                                                   scale=GK ** -0.5 if i < GF else 1.0)
                        rd.free(ins, "qk", i)
                    act.wait_ge(sem("vec_landed"), 16)
                    act.wait_ge(sem("z_filled"), 1)
                    for f in range(GF):
                        nc.scalar.activation(gf["z"][:, f, :], M[1][:, f * T:(f + 1) * T], ACT.Identity,
                                             bias=vcol(va, VEC_A, "b_a", f)).then_inc(sem("z_made"), 1)
                    act.wait_ge(sem("z_made"), GF)
                    nc.scalar.activation(flat["za"], flat["z"], ACT.Abs).then_inc(sem("act_gate"), 1)
                    act.wait_ge(sem("act_gate"), 1)
                    nc.scalar.activation(flat["za"], flat["za"], ACT.Exp, scale=-1.0).then_inc(sem("act_gate"), 1)
                    act.wait_ge(sem("act_gate"), 2)
                    nc.scalar.activation(flat["za"], flat["za"], ACT.Ln, bias=1.0).then_inc(sem("act_gate"), 1)
                    for i in range(TT):
                        ins = nc.scalar.activation(v[:, i, :], rd.full("v", i)[:, :], ACT.Copy)
                        rd.free(ins, "v", i)
                    act.wait_ge(sem("bc_made"), GF)
                    nc.scalar.activation(flat["ep"], flat["bc"], ACT.Exp, scale=1.0 / 16.0).then_inc(sem("ep_made"), 1)
                    nc.scalar.activation(flat["en"], flat["bc"], ACT.Exp, scale=-1.0 / 16.0).then_inc(sem("en_made"), 1)
                    act.wait_ge(sem("bd_made"), GF)
                    nc.scalar.activation(flat["ed"], flat["ed"], ACT.Exp, scale=1.0 / 16.0).then_inc(sem("ed_made"), 1)
                    for i in range(CF):
                        ins = nc.scalar.activation(r[:, i, :], rd.full("r", i)[:, 0:T], ACT.Silu)
                        rd.free(ins, "r", i)
                    for i in range(4):
                        ins = nc.scalar.activation(xk[:, i, :], rd.full("xk", i)[:, 0:T], ACT.Copy)
                        rd.free(ins, "xk", i)
                    act.wait_ge(sem("kdt_filled"), 1)
                    nc.scalar.activation(cut(A_MEM, "kdt"), M[2][:, :], ACT.Copy).then_inc(sem("kdt_read"), 1)
                    for i in range(4, 8):
                        ins = nc.scalar.activation(xk[:, i, :], rd.full("xk", i)[:, 0:T], ACT.Copy)
                        rd.free(ins, "xk", i)
                    for i in range(4):
                        ins = nc.scalar.activation(xv[:, i % 2, (i // 2) * 512:(i // 2 + 1) * 512],
                                                   rd.full("xv", i)[:, :], ACT.Copy)
                        rd.free(ins, "xv", i)
                    for h in range(GH):
                        bank = rd.full("o", h)
                        nc.scalar.activation(sq[:, 4 + h, :], bank[:, 0:T], ACT.Square).then_inc(sem("osq_made"), 1)
                        ins = nc.scalar.activation(o[:, h, :], bank[:, 0:T], ACT.Copy)
                        rd.free(ins, "o", h)
                    for p in range(2):
                        act.wait_ge(sem("rms_filled"), 2 * p + 2)
                        nc.scalar.activation(rs[:, 2 * p:2 * p + 2, :].rearrange("p h t -> p (h t)"), M[1 + p][:, :],
                                             ACT.Sqrt, scale=1.0 / GV, bias=eps[:, 0:1]).then_inc(sem("rms_sd"), 1)
                    norm_act(act, "cln", CF, mix, va, VEC_A, "cln_g", "cln_b", func=ACT.Silu)
                    norm_act(act, "ln1", KD, x3, va, VEC_A, "ln1_g", "ln1_b")
                    for i in range(KD):
                        ins = nc.scalar.activation(qx[:, i, :], rd.full("xq", i)[:, 0:T], ACT.Copy,
                                                   scale=(D // XH) ** -0.5)
                        rd.free(ins, "xq", i)
                    for i in range(8):
                        bank = rd.full("sc", i)
                        act.wait_ge(sem("nmax_made"), i + 1)
                        ins = nc.scalar.activation(px[:, i, :], bank[:, 0:T], ACT.Exp, bias=nmax[:, i:i + 1],
                                                   accum_out=rsum[:, i:i + 1])
                        rd.free(ins, "sc", i)
                    for h in range(XH):
                        ins = nc.scalar.activation(ptx[:, h, :, :].rearrange("p m t -> p (m t)"),
                                                   rd.full("pt", h)[:, :], ACT.Copy)
                        rd.free(ins, "pt", h)
                    norm_act(act, "ln2", KD, x3, va, VEC_A, "ln2_g", "ln2_b")
                    for i in range(KF):
                        if i >= 4:
                            rd.read_wait("fi", 2 * i - 7)
                        ins = nc.scalar.activation(sg[:, i % 4, :], rd.full("fi", 2 * i)[:, 0:T], ACT.Silu)
                        rd.free(ins, "fi", 2 * i)
                    norm_act(act, "ln3", KD, x3, va, VEC_A, "ln3_g", "ln3_b")

                @block.gpsimd
                def _(pool):
                    nc.gpsimd.memset(glu[:, :, 0:TAPS - 1], 0.0).then_inc(sem("pad_set"), 1)
                    nc.gpsimd.memset(cut(A_MEM, "att"), 0.0).then_inc(sem("att_zeroed"), 1)
                    rd = Reader(pool, A_TILES)
                    for i in range(4):
                        rd.read_wait("qk", i)
                    pool.wait_ge(sem("ed_made"), 1)
                    nc.gpsimd.tensor_tensor(flat["kd"], flat["k"], flat["ed"], ALU.mult).then_inc(sem("kd_made"), 1)
                    nc.gpsimd.tensor_tensor(flat["qe"], flat["q"], flat["ep"], ALU.mult).then_inc(sem("qe_made"), 1)
                    nc.gpsimd.tensor_tensor(flat["ke"], flat["k"], flat["en"], ALU.mult).then_inc(sem("qe_made"), 1)

                @block.vector
                def _(dve):
                    rd = Reader(dve, A_TILES)
                    conv_steps = 0

                    def glu_tile(i):
                        rd.read_wait("glu", 2 * i)
                        ins = nc.vector.tensor_tensor(glu[:, i, TAPS - 1:], rd.full("glu", 2 * i + 1)[:, 0:T],
                                                      sig[:, i, :], ALU.mult)
                        rd.free(ins, "glu", 2 * i + 1)

                    def conv_pair(f0):
                        nonlocal conv_steps
                        for i in (f0, f0 + 1):
                            rd.read_wait("glu", 2 * i + 1)
                        for j in range(TAPS):
                            for i in (f0, f0 + 1):
                                if j == 0:
                                    ins = nc.vector.tensor_scalar(cy[:, i, :], glu[:, i, 0:T], conv_w[:, i, 0:1],
                                                                  vcol(va, VEC_A, "conv_b", i), ALU.mult, ALU.add)
                                else:
                                    dve.wait_ge(sem("tap_added"), conv_steps - 1)
                                    ins = nc.vector.scalar_tensor_tensor(
                                        out=cy[:, i, :], in0=glu[:, i, j:j + T], scalar=conv_w[:, i, j:j + 1],
                                        in1=cy[:, i, :], op0=ALU.mult, op1=ALU.add)
                                conv_steps += 1
                                if j == TAPS - 1:
                                    ins.then_inc(sem("conv_made"), 1)
                                else:
                                    ins.then_inc(sem("tap_added"), 1)
                        conv_steps -= 2

                    dve.wait_ge(sem("vec_landed"), 16)
                    dve.wait_ge(sem("pad_set"), 1)
                    for i in range(CF):
                        glu_tile(i)
                    dve.wait_ge(sem("act_gate"), 3)
                    nc.vector.tensor_scalar(flat["z"], flat["z"], 0.0, None, ALU.min).then_inc(sem("gate"), 1)
                    dve.wait_ge(sem("gate"), 1)
                    nc.vector.tensor_tensor(flat["z"], flat["z"], flat["za"], ALU.subtract).then_inc(sem("gate"), 1)
                    dve.wait_ge(sem("gate"), 2)
                    for f in range(GF):
                        nc.vector.tensor_tensor_scan(gf["bc"][:, f, :], cst[:, CONST["scan"]], gf["z"][:, f, :], 0.0,
                                                     ALU.mult, ALU.add).then_inc(sem("bc_made"), 1)
                    dve.wait_ge(sem("bc_made"), GF)
                    bcc = cut(A_MEM, "bc", "p (c t) -> p c t", t=CHUNK)
                    edc = cut(A_MEM, "ed", "p (c t) -> p c t", t=CHUNK)
                    half = GF * NCHUNK // 2
                    for i in range(2):
                        cs = slice(i * half, (i + 1) * half)
                        nc.vector.tensor_tensor(edc[:, cs, :],
                                                bcc[:, cs, CHUNK - 1:CHUNK].broadcast_to([P, half, CHUNK]),
                                                bcc[:, cs, :], ALU.subtract).then_inc(sem("bd_made"), 1)
                    conv_pair(0)
                    conv_pair(2)
                    dve.wait_ge(sem("att_zeroed"), 1)
                    for n in range(8):
                        dve.wait_ge(sem("att_filled"), n // 4 + 1)
                        nc.vector.copy_predicated(att[:, n, :], mask[:, :], M[n // 4][:, (n % 4) * P:(n % 4 + 1) * P]
                                                  ).then_inc(sem("att_masked"), 1)
                    ep4 = cut(A_MEM, "ep", "p (f t) -> p f t", f=GF)
                    dve.wait_ge(sem("ep_made"), 1)
                    ins = nc.vector.tensor_copy(st[:, 0, :, :].rearrange("p f n -> p (f n)"),
                                                rd.full("upd", 0)[:, 0:GF * GV])
                    rd.free(ins, "upd", 0)
                    for c in range(1, NCHUNK - 1):
                        bank = rd.full("upd", c)
                        rd.read_wait("upd", c - 1)
                        if c > 1:
                            dve.wait_ge(sem("state_half"), c - 1)
                        nc.vector.scalar_tensor_tensor(
                            out=st[:, c, 0, :], in0=st[:, c - 1, 0, :],
                            scalar=ep4[:, 0, (c + 1) * CHUNK - 1:(c + 1) * CHUNK], in1=bank[:, 0:GV],
                            op0=ALU.mult, op1=ALU.add).then_inc(sem("state_half"), 1)
                        ins = nc.vector.scalar_tensor_tensor(
                            out=st[:, c, 1, :], in0=st[:, c - 1, 1, :],
                            scalar=ep4[:, 1, (c + 1) * CHUNK - 1:(c + 1) * CHUNK], in1=bank[:, GV:2 * GV],
                            op0=ALU.mult, op1=ALU.add)
                        rd.free(ins, "upd", c)
                    for p in range(2):
                        dve.wait_ge(sem("rms_sd"), p + 1)
                        pair = rs[:, 2 * p:2 * p + 2, :].rearrange("p h t -> p (h t)")
                        nc.vector.reciprocal(pair, pair).then_inc(sem("rms_r"), 1)
                    rd.read_wait("o", GH - 1)
                    dve.wait_ge(sem("rms_r"), 2)
                    for h in range(GH):
                        rd.read_wait("o", h)
                        nc.vector.tensor_tensor(o[:, h, :], o[:, h, :], rs[:, h, :], ALU.mult
                                                ).then_inc(sem("o_scaled"), 1)
                    for h in range(GH):
                        dve.wait_ge(sem("o_scaled"), h + 1)
                        rd.read_wait("r", h)
                        nc.vector.scalar_tensor_tensor(out=mix[:, CF + h, :], in0=o[:, h, :],
                                                       scalar=vcol(va, VEC_A, "gla_g"), in1=r[:, h, :],
                                                       op0=ALU.mult, op1=ALU.mult).then_inc(sem("gated"), 1)
                    norm_dve(dve, "cln", cy, CF)

                    def residual(stage, ln):
                        for f in range(KD):
                            bank = rd.full(stage, f)
                            ins = nc.vector.scalar_tensor_tensor(out=x3[:, f, :], in0=x3[:, f, :], scalar=ALPHA,
                                                                 in1=bank[:, 0:T], op0=ALU.mult, op1=ALU.add)
                            rd.free(ins, stage, f)
                        for f in range(KD):
                            rd.read_wait(stage, f)
                        norm_dve(dve, ln, x3, KD)

                    residual("mix", "ln1")
                    for i in range(8):
                        bank = rd.full("sc", i)
                        nc.vector.tensor_reduce(nmax[:, i:i + 1], bank[:, 0:T], AX_X, ALU.max, negate=True
                                                ).then_inc(sem("nmax_made"), 1)
                    for i in range(8):
                        rd.read_wait("sc", i)
                        nc.vector.reciprocal(rinv[:, i:i + 1], rsum[:, i:i + 1]).then_inc(sem("rinv_made"), 1)
                        dve.wait_ge(sem("rinv_made"), i + 1)
                        nc.vector.tensor_scalar(px[:, i, :], px[:, i, :], rinv[:, i:i + 1], None, ALU.mult
                                                ).then_inc(sem("px_made"), 1)
                    for f in range(KD):
                        ins = nc.vector.tensor_copy(oxx[:, f, :], rd.full("ox", f)[:, 0:T])
                        rd.free(ins, "ox", f)
                    residual("xo", "ln2")
                    for i in range(KF):
                        rd.read_wait("fi", 2 * i)
                        ins = nc.vector.tensor_tensor(hid[:, i, :], rd.full("fi", 2 * i + 1)[:, 0:T], sg[:, i % 4, :],
                                                      ALU.mult)
                        rd.free(ins, "fi", 2 * i + 1)
                    residual("fo", "ln3")
                    dve.wait_ge(sem("mod_filled"), 12)
                    dst = modT[:, bass.ds(layer * 96, 96)].rearrange("p (j c) -> p j c", c=2)
                    nc.vector.tensor_tensor(dst, M[3][:, 0:96].rearrange("p (j c) -> p j c", c=2),
                                            va[:, VEC_A["b_mod"]].unsqueeze(2).broadcast_to([P, 48, 2]), ALU.add)
            clear_semaphores()

        lng, lnb = VEC_B["ln_g"].start, VEC_B["ln_b"].start
        POST = {"g": slice(lng, lng + 32), "b": slice(lnb, lnb + 32)}
        ht = memT[:, :].rearrange("p (a n) -> p a n", a=TT)
        hp = cut(Q_MEM, "hp", "p (f t) -> p f t", f=KD)
        pq = cut(Q_MEM, "pq", "p (j t) -> p j t", j=16)
        s12 = cut(P_MEM, "s12", "p (a n) -> p a n", a=TT)

        def mod_part(l, part, f, c=0):
            return mod4[:, l, part * KD + f, c:c + 1]

        def peer_prep_pe(e, rd):
            for f in range(KD):
                e.pe.wait_ge(sem("hp_made"), f + 1)
            for i in range(2):
                e.feature_tiles(e.panel("pq", i), "pq", 4 * i, 4, KD, hp, T)
            for i in range(4):
                bank = e.bank("ht", i)
                for j in range(4):
                    f = (i % 2) * 4 + j
                    ins = nc.tensor.transpose(bank[:, j * P:(j + 1) * P], hp[:, f, (i // 2) * P:(i // 2 + 1) * P],
                                              ident)
                e.filled(ins, "ht", i)
            for i in range(2, 4):
                e.feature_tiles(e.panel("pq", i), "pq", 4 * i, 4, KD, hp, T)
            keys = e.panel("pk", 0)
            for i in range(8):
                a, g = i // 4, i % 4
                for j in range(4):
                    rd.read_wait("pq", 4 * g + j)
                bank = e.bank("ps", i)
                for j in range(4):
                    n = 4 * g + j
                    ins = nc.tensor.matmul(bank[:, j * P:(j + 1) * P], pq[:, n, a * P:(a + 1) * P],
                                           keys[:, n * P:(n + 1) * P], start=True, stop=True)
                e.filled(ins, "ps", i)

        def peer_prep_act(act, rd, l, ln):
            for f in range(KD):
                act.wait_ge(sem(f"{ln}_out"), f + 1)
                nc.scalar.activation(hp[:, f, :], x3[:, f, :], ACT.Identity, scale=mod_part(l, 4, f),
                                     bias=mod_part(l, 3, f)).then_inc(sem("hp_made"), 1)
            for i in range(16):
                ins = nc.scalar.activation(pq[:, i, :], rd.full("pq", i)[:, 0:T], ACT.Copy)
                rd.free(ins, "pq", i)

        def peer_prep_dve(dve, rd):
            for i in range(4):
                ins = nc.vector.tensor_copy(ht[:, i // 2, (i % 2) * 512:(i % 2 + 1) * 512], rd.full("ht", i)[:, :])
                rd.free(ins, "ht", i)
            for i in range(8):
                ins = nc.vector.tensor_copy(s12[:, i // 4, (i % 4) * 512:(i % 4 + 1) * 512], rd.full("ps", i)[:, :])
                rd.free(ins, "ps", i)

        def gated_act(act, rd, stage, l, part):
            gated = sq
            for f in range(KD):
                ins = nc.scalar.activation(gated[:, f, :], rd.full(stage, f)[:, 0:T], ACT.Copy,
                                           scale=mod_part(l, part, f))
                rd.free(ins, stage, f)

        def gated_residual_dve(dve, wait, signal):
            for f in range(KD):
                wait(f)
                nc.vector.scalar_tensor_tensor(out=x3[:, f, :], in0=x3[:, f, :], scalar=ALPHA, in1=sq[:, f, :],
                                               op0=ALU.mult, op1=ALU.add).then_inc(sem(signal), 1)
            dve.wait_ge(sem(signal), KD)

        hh = cut(B_MEM, "h", "p (f t) -> p f t", f=KD)
        cq = cut(B_MEM, "cq", "p (f t) -> p f t", f=3)
        ckv = cut(B_MEM, "ckv", "p (f t) -> p f t", f=2)
        kr = cut(B_MEM, "kr", "p (f t) -> p f t", f=2)
        kro = cut(B_MEM, "kro", "p (f t) -> p f t", f=2)
        qr = cut(B_MEM, "qr", "p (f t) -> p f t", f=4)
        qro = cut(B_MEM, "qro", "p (f t) -> p f t", f=4)
        qn = cut(B_MEM, "qn", "p (f t) -> p f t", f=MH)
        kn = cut(B_MEM, "kn", "p (f t) -> p f t", f=MH)
        vm = cut(B_MEM, "vm", "p (m n) -> p m n", m=4)
        tm = cut(B_MEM, "tmp", "p (f t) -> p f t", f=2)
        pb = cut(B_MEM, "p", "p (a t) -> p a t", a=2)
        ptb = cut(B_MEM, "pt", "p (a m t) -> p m a t", a=2, m=4)
        ptb_flat = cut(B_MEM, "pt", "p (a n) -> p a n", a=2)
        oxb = arena[:, B_OX:B_OX + KD * T].rearrange("p (f t) -> p f t", f=KD)
        cos, sin = cst[:, CONST["cos"]], cst[:, CONST["sin"]]
        MSCALE = (NOPE + ROPE) ** -0.5
        ROT = MH * ROPE // 2 // P

        with nc.Block() as block:
            @block.sync
            def _(sp):
                sp.dma_start(hh[:, :, T:2 * T], acts[2].rearrange("p (f t) -> p f t", f=KD)
                             ).then_inc(sem("ctx_landed"), 16)
                stream(sp, B_PANELS, B_TILES, DEPTH * len(A_PANELS), True)

            @block.tensor
            def _(pe):
                e = PE(pe, B_PANELS, B_TILES)
                rd = Reader(pe, B_TILES)
                pe.wait_ge(sem("h_made"), 2 * KD)
                w = e.panel("zi", 0)
                e.feature_tiles(w, "zi", 0, 3, KD, hh, T)
                e.feature_tiles(w[:, 3 * KD * P:], "zi", 3, 1, KD, hh, 2 * T)
                e.feature_tiles(e.panel("zi", 1), "zi", 4, 3, KD, hh, 2 * T)
                for f in range(3):
                    pe.wait_ge(sem("lsq_made"), f + 1)
                    ins = nc.tensor.matmul(M[0][:, 0:T], ones[:, :], sq[:, f, :], start=(f == 0), stop=(f == 2))
                ins.then_inc(sem("rms_filled"), 1)
                for f in range(2):
                    pe.wait_ge(sem("lsq_made"), f + 4)
                    ins = nc.tensor.matmul(M[1][:, :], ones[:, :],
                                           sq[:, 3 + 2 * f:5 + 2 * f, :].rearrange("p a t -> p (a t)"),
                                           start=(f == 0), stop=(f == 1))
                ins.then_inc(sem("rms_filled"), 1)
                pe.wait_ge(sem("cq_normed"), 3)
                for i in range(2):
                    e.feature_tiles(e.panel("uq", i), "uq", 6 * i, 6, 3, cq, T)
                pe.wait_ge(sem("ckv_normed"), 2)
                w = e.panel("ukv", 0)
                e.feature_tiles(w, "kn", 0, MH, 2, ckv, 2 * T)
                for c in range(2):
                    e.token_tiles(w, "vm", 4 * c, 4, 2, ckv, width=D, off=MH * 2 * P + c * 512)
                pe.wait_ge(sem("q_rotated"), 2 * ROT)
                pe.wait_ge(sem("k_rotated"), 2)

                def scores(h):
                    rd.read_wait("uq", h)
                    rd.read_wait("kn", h)
                    rows = slice((h % 4) * 32, (h % 4 + 1) * 32)
                    for a in range(TT):
                        bank = e.bank("sc", 2 * h + a)
                        cols = slice(a * P, (a + 1) * P)
                        nc.tensor.matmul(bank[:, :], qn[:, h, cols], kn[:, h, :], start=True, stop=False)
                        for k in range(2):
                            ins = nc.tensor.matmul(bank[:, :], qro[rows, k * ROT + h // 4, cols], kro[rows, k, :],
                                                   start=False, stop=(k == 1),
                                                   tile_position=((h % 4) * 32, 0))
                        e.filled(ins, "sc", 2 * h + a)

                def values(h):
                    for a in range(TT):
                        pe.wait_ge(sem("p_made"), 2 * h + a + 1)
                        bank = e.bank("pt", 2 * h + a)
                        for m in range(4):
                            ins = nc.tensor.transpose(bank[:, m * P:(m + 1) * P], pb[:, a, m * P:(m + 1) * P], ident)
                        e.filled(ins, "pt", 2 * h + a)
                    for a in range(TT):
                        rd.read_wait("pt", 2 * h + a)
                    bank = e.bank("ox", h)
                    for a in range(TT):
                        for m in range(4):
                            ins = nc.tensor.matmul(bank[:, a * P:(a + 1) * P], vm[:, m, h * VD:(h + 1) * VD],
                                                   ptb[:, m, a, :], start=(m == 0), stop=(m == 3))
                    e.filled(ins, "ox", h)

                for i in range(8):
                    rd.read_wait("vm", i)
                for h in range(MH):
                    scores(h)
                    if h:
                        values(h - 1)
                values(MH - 1)
                for h in range(MH):
                    rd.read_wait("ox", h)
                for i in range(2):
                    e.feature_tiles(e.panel("wo", i), "wo", 4 * i, 4, KD, oxb, T)
                norm_pe(pe, "lnb", lambda f: pe.wait_ge(sem("res_made"), f + 1), x3, KD)
                peer_prep_pe(e, rd)

            @block.scalar
            def _(act):
                rd = Reader(act, B_TILES)
                act.wait_ge(sem("mod_ready"), 1)
                act.wait_ge(sem("ctx_landed"), 16)
                for f in range(KD):
                    nc.scalar.activation(hh[:, f, 0:T], x3[:, f, :], ACT.Identity, scale=mod_part(0, 1, f),
                                         bias=mod_part(0, 0, f)).then_inc(sem("h_made"), 1)
                    nc.scalar.activation(hh[:, f, T:2 * T], hh[:, f, T:2 * T], ACT.Identity,
                                         scale=mod_part(0, 1, f, 1), bias=mod_part(0, 0, f, 1)
                                         ).then_inc(sem("h_made"), 1)
                for i in range(3):
                    bank = rd.full("zi", i)
                    nc.scalar.activation(sq[:, i, :], bank[:, 0:T], ACT.Square).then_inc(sem("lsq_made"), 1)
                    rd.free(nc.scalar.activation(cq[:, i, :], bank[:, 0:T], ACT.Copy), "zi", i)
                for i in range(2):
                    bank = rd.full("zi", 3 + i)
                    nc.scalar.activation(sq[:, 3 + 2 * i:5 + 2 * i, :].rearrange("p a t -> p (a t)"), bank[:, :],
                                         ACT.Square).then_inc(sem("lsq_made"), 1)
                    rd.free(nc.scalar.activation(ckv[:, i, :], bank[:, :], ACT.Copy), "zi", 3 + i)
                for i in range(2):
                    rd.free(nc.scalar.activation(kr[:, i, :], rd.full("zi", 5 + i)[:, :], ACT.Copy), "zi", 5 + i)
                act.wait_ge(sem("rms_filled"), 1)
                nc.scalar.activation(sd, M[0][:, 0:T], ACT.Sqrt, scale=1.0 / QL, bias=eps[:, 1:2]
                                     ).then_inc(sem("rms_sd"), 1)
                act.wait_ge(sem("rms_filled"), 2)
                nc.scalar.activation(tm[:, 0, :], M[1][:, :], ACT.Sqrt, scale=1.0 / KVL, bias=eps[:, 1:2]
                                     ).then_inc(sem("rms_sd"), 1)
                for i in range(12):
                    dst = qn[:, i, :] if i < MH else qr[:, i - MH, :]
                    rd.free(nc.scalar.activation(dst, rd.full("uq", i)[:, 0:T], ACT.Copy), "uq", i)
                for i in range(MH):
                    rd.free(nc.scalar.activation(kn[:, i, :], rd.full("kn", i)[:, :], ACT.Copy), "kn", i)

                def softmax(h):
                    for a in range(TT):
                        n = 2 * h + a
                        bank = rd.full("sc", n)
                        act.wait_ge(sem("nmax_scaled"), n + 1)
                        if h:
                            rd.full("pt", n - 2)
                        ins = nc.scalar.activation(pb[:, a, :], bank[:, :], ACT.Exp, scale=MSCALE,
                                                   bias=nmax[:, n:n + 1], accum_out=rsum[:, n:n + 1])
                        rd.free(ins, "sc", n)

                for h in range(MH):
                    softmax(h)
                    for a in range(TT):
                        n = 2 * h + a
                        if h:
                            rd.full("ox", h - 1)
                        rd.free(nc.scalar.activation(ptb_flat[:, a, :], rd.full("pt", n)[:, :], ACT.Copy), "pt", n)
                gated_act(act, rd, "wo", 0, 2)
                norm_act(act, "lnb", KD, x3, vb, POST, "g", "b", off=0)
                peer_prep_act(act, rd, 0, "lnb")

            @block.vector
            def _(dve):
                rd = Reader(dve, B_TILES)
                scales = modT[:, :].rearrange("p (l q j) -> p l q j", l=DEPTH, q=6)
                for part in (1, 4):
                    ins = nc.vector.tensor_scalar(scales[:, :, part, :], scales[:, :, part, :], 1.0, None, ALU.add)
                    ins.then_inc(sem("mod_half" if part == 1 else "mod_ready"), 1)
                dve.wait_ge(sem("mod_ready"), 1)
                dve.wait_ge(sem("mod_half"), 1)

                def rotate(out1, out2, x1, x2, c, s, signal):
                    n = x1.shape[-1]
                    t1, t2 = xc[:, 0:2, :].rearrange("p a t -> p (a t)")[:, 0:n], \
                        xc[:, 2:4, :].rearrange("p a t -> p (a t)")[:, 0:n]
                    nonlocal turned
                    for o_, a_, b_, op in ((out1, c, s, ALU.subtract), (out2, s, c, ALU.add)):
                        nc.vector.tensor_tensor(t1, x1, a_, ALU.mult).then_inc(sem("turned"), 1)
                        nc.vector.tensor_tensor(t2, x2, b_, ALU.mult).then_inc(sem("turned"), 1)
                        turned += 2
                        dve.wait_ge(sem("turned"), turned)
                        signalled[signal] = signalled.get(signal, 0) + 1
                        nc.vector.tensor_tensor(o_, t1, t2, op).then_inc(sem(signal), 1)
                        dve.wait_ge(sem(signal), signalled[signal])

                turned, signalled = 0, {}
                for i in range(2):
                    rd.read_wait("zi", 5 + i)
                rotate(kro[:, 0, :], kro[:, 1, :], kr[:, 0, :], kr[:, 1, :], cos, sin, "k_rotated")
                dve.wait_ge(sem("rms_sd"), 1)
                nc.vector.reciprocal(rstd, sd).then_inc(sem("rms_r"), 1)
                dve.wait_ge(sem("rms_r"), 1)
                for i in range(3):
                    rd.read_wait("zi", i)
                    nc.vector.scalar_tensor_tensor(out=cq[:, i, :], in0=cq[:, i, :], scalar=vcol(vb, VEC_B, "q_norm", i),
                                                   in1=rstd, op0=ALU.mult, op1=ALU.mult
                                                   ).then_inc(sem("cq_normed"), 1)
                dve.wait_ge(sem("rms_sd"), 2)
                nc.vector.reciprocal(tm[:, 1, :], tm[:, 0, :]).then_inc(sem("rms_r"), 1)
                dve.wait_ge(sem("rms_r"), 2)
                for i in range(2):
                    rd.read_wait("zi", 3 + i)
                    nc.vector.scalar_tensor_tensor(out=ckv[:, i, :], in0=ckv[:, i, :],
                                                   scalar=vcol(vb, VEC_B, "kv_norm", i), in1=tm[:, 1, :],
                                                   op0=ALU.mult, op1=ALU.mult).then_inc(sem("ckv_normed"), 1)
                for i in range(ROT):
                    rd.read_wait("uq", MH + i)
                    rd.read_wait("uq", MH + ROT + i)
                    rotate(qro[:, i, :], qro[:, ROT + i, :], qr[:, i, :], qr[:, ROT + i, :], cos[:, 0:T], sin[:, 0:T],
                           "q_rotated")
                for i in range(8):
                    rd.free(nc.vector.tensor_copy(vm[:, i % 4, (i // 4) * 512:(i // 4 + 1) * 512],
                                                  rd.full("vm", i)[:, :]), "vm", i)

                def peak(h):
                    for a in range(TT):
                        n = 2 * h + a
                        nc.vector.tensor_reduce(nmax[:, n:n + 1], rd.full("sc", n)[:, :], AX_X, ALU.max, negate=True
                                                ).then_inc(sem("nmax_made"), 1)
                        dve.wait_ge(sem("nmax_made"), n + 1)
                        nc.vector.tensor_scalar(nmax[:, n:n + 1], nmax[:, n:n + 1], MSCALE, None, ALU.mult
                                                ).then_inc(sem("nmax_scaled"), 1)

                for h in range(MH):
                    peak(h)
                    for a in range(TT):
                        n = 2 * h + a
                        rd.read_wait("sc", n)
                        nc.vector.reciprocal(rinv[:, n:n + 1], rsum[:, n:n + 1]).then_inc(sem("rinv_made"), 1)
                        dve.wait_ge(sem("rinv_made"), n + 1)
                        nc.vector.tensor_scalar(pb[:, a, :], pb[:, a, :], rinv[:, n:n + 1], None, ALU.mult
                                                ).then_inc(sem("p_made"), 1)
                    if h:
                        rd.free(nc.vector.tensor_copy(oxb[:, h - 1, :], rd.full("ox", h - 1)[:, 0:T]), "ox", h - 1)
                rd.free(nc.vector.tensor_copy(oxb[:, MH - 1, :], rd.full("ox", MH - 1)[:, 0:T]), "ox", MH - 1)
                gated_residual_dve(dve, lambda f: rd.read_wait("wo", f), "res_made")
                norm_dve(dve, "lnb", x3, KD)
                peer_prep_dve(dve, rd)
        clear_semaphores()

        slot = cut(P_MEM, "ring", "p (s n) -> p s n", s=RING)
        ht_now = cut(P_MEM, "hc")
        sc = cut(P_MEM, "sc", "p (h b n) -> p h b n", h=PH, b=2)
        wk = cut(P_MEM, "wk", "p (b n) -> p b n", b=2)
        v16 = cut(P_MEM, "v16", "p (b k) -> p b k", b=2)
        i16 = cut(P_MEM, "i16").bitcast(U32).rearrange("p (b k) -> p b k", b=2)
        i16f = cut(P_MEM, "if", "p (b k) -> p b k", b=2)
        cand = cut(P_MEM, "cand", "p (i j) -> p i j", i=TOPK)
        cw = cut(P_MEM, "cw")
        top = cut(P_MEM, "top")
        pos = cut(P_MEM, "pos").bitcast(U32)
        ab = cut(P_MEM, "ab").bitcast(U32).rearrange("p (b k) -> p b k", b=2)
        abf = cut(P_MEM, "abf", "p (b k) -> p b k", b=2)
        oh = cut(P_MEM, "oh", "p (k i) -> p k i", k=TOPK)
        selected = cut(P_MEM, "sel", "p (b k) -> p b k", b=2)
        idf = cut(P_MEM, "idf")
        idx = cut(P_MEM, "idx").bitcast(U32)
        gate = cut(P_MEM, "g")
        gs = cut(P_MEM, "gs")
        dot, gelu, coef = cut(P_MEM, "dot"), cut(P_MEM, "act"), cut(P_MEM, "cf")
        acc = cut(P_MEM, "acc", "p (b n) -> p b n", b=2)
        iota = cst[:, CONST["iota"]]
        NSLOT = PH * TOPK
        PAIR = 2

        def peer(l):
            with nc.Fori(0, TT) as a:
                with nc.Block() as block:
                    @block.gpsimd
                    def _(pool):
                        for s in range(NSLOT):
                            if s % TOPK == 0:
                                pool.wait_ge(sem("idx_made"), s // TOPK + 1)
                            if s >= RING:
                                pool.wait_ge(sem("row_used"), s - RING + 1)
                            pool.indirect_dma_start(slot[:, s % RING, :], None, tables,
                                                    bass.IndirectOffsetOnAxis(idx[:, s:s + 1], 0)
                                                    ).then_inc(sem(f"row_landed{s % RING}"), 16)

                    @block.scalar
                    def _(act):
                        def softmax(h):
                            act.wait_ge(sem("top_made"), h + 1)
                            nc.scalar.activation(gate[:, h * TOPK:(h + 1) * TOPK], top, ACT.Exp, bias=gs[:, 0:1],
                                                 accum_out=gs[:, 1:2]).then_inc(sem("gate_exp"), 1)
                        softmax(0)
                        for s in range(0, NSLOT, PAIR):
                            if s % TOPK == 0 and s // TOPK + 1 < PH:
                                softmax(s // TOPK + 1)
                            act.wait_ge(sem("dot_made"), s + PAIR)
                            nc.scalar.activation(gelu[:, s:s + PAIR], dot[:, s:s + PAIR], ACT.Gelu
                                                 ).then_inc(sem("gelu_made"), 1)

                    @block.vector
                    def _(dve):
                        done = 0

                        def chain(ins):
                            nonlocal done
                            done += 1
                            ins.then_inc(sem("step"), 1)
                            dve.wait_ge(sem("step"), done)

                        def best16(values, index, src, work):
                            chain(nc.vector.max(values[:, 0:8], src))
                            chain(nc.vector.max_index(index[:, 0:8], values[:, 0:8], src))
                            chain(nc.vector.match_replace(work, values[:, 0:8], src, NEG))
                            chain(nc.vector.max(values[:, 8:16], work))
                            chain(nc.vector.max_index(index[:, 8:16], values[:, 8:16], work))

                        def select(h):
                            for b in range(2):
                                best16(v16[:, b, :], i16[:, b, :], sc[:, h, b, :], wk[:, b, :])
                            chain(nc.vector.tensor_copy(i16f, i16))
                            chain(nc.vector.tensor_tensor(cand, v16[:, 0, :].unsqueeze(2).broadcast_to([P, TOPK, TOPK]),
                                                          v16[:, 1, :].unsqueeze(1).broadcast_to([P, TOPK, TOPK]),
                                                          ALU.add))
                            if h:
                                dve.wait_ge(sem("gate_exp"), h)
                            best16(top, pos, cand.rearrange("p i j -> p (i j)"), cw)
                            nc.vector.tensor_scalar(gs[:, 0:1], top[:, 0:1], -1.0, None, ALU.mult
                                                    ).then_inc(sem("top_made"), 1)
                            chain(nc.vector.tensor_scalar(ab[:, 0, :], pos, 4, None, ALU.logical_shift_right))
                            chain(nc.vector.tensor_scalar(ab[:, 1, :], pos, 15, None, ALU.bitwise_and))
                            chain(nc.vector.tensor_copy(abf, ab))
                            for b in range(2):
                                chain(nc.vector.tensor_tensor(oh, abf[:, b, :].unsqueeze(2).broadcast_to([P, TOPK, TOPK]),
                                                              iota.unsqueeze(1).broadcast_to([P, TOPK, TOPK]),
                                                              ALU.is_equal))
                                chain(nc.vector.tensor_tensor(oh, oh,
                                                              i16f[:, b, :].unsqueeze(1).broadcast_to([P, TOPK, TOPK]),
                                                              ALU.mult))
                                chain(nc.vector.tensor_reduce(selected[:, b, :], oh, AX_X, ALU.add))
                            chain(nc.vector.scalar_tensor_tensor(out=idf, in0=selected[:, 0, :], scalar=float(NK),
                                                                 in1=selected[:, 1, :], op0=ALU.mult, op1=ALU.add))
                            nc.vector.tensor_scalar(idx[:, h * TOPK:(h + 1) * TOPK], idf, float(l * NEXP), None, ALU.add
                                                    ).then_inc(sem("idx_made"), 1)
                            dve.wait_ge(sem("idx_made"), h + 1)
                            dve.wait_ge(sem("gate_exp"), h + 1)
                            chain(nc.vector.reciprocal(gs[:, 2:3], gs[:, 1:2]))
                            chain(nc.vector.tensor_scalar(gate[:, h * TOPK:(h + 1) * TOPK],
                                                          gate[:, h * TOPK:(h + 1) * TOPK], gs[:, 2:3], None, ALU.mult))

                        def dots(s0):
                            for s in range(s0, s0 + PAIR):
                                dve.wait_ge(sem(f"row_landed{s % RING}"),
                                            (a + TT * l) * (16 * NSLOT // RING) + 16 * (s // RING + 1))
                                u = slot[:, s % RING, 0:D]
                                nc.vector.tensor_tensor_reduce(out=u, in0=u, in1=ht_now, scale=1.0, scalar=0.0,
                                                               op0=ALU.mult, op1=ALU.add, accum_out=dot[:, s:s + 1]
                                                               ).then_inc(sem("dot_made"), 1)

                        def accumulate(s0):
                            dve.wait_ge(sem("gelu_made"), s0 // PAIR + 1)
                            chain(nc.vector.tensor_tensor(coef[:, s0:s0 + PAIR], gelu[:, s0:s0 + PAIR],
                                                          gate[:, s0:s0 + PAIR], ALU.mult))
                            for s in range(s0, s0 + PAIR):
                                v_row, into = slot[:, s % RING, D:2 * D], acc[:, s % 2, :]
                                if s < 2:
                                    ins = nc.vector.tensor_scalar(into, v_row, coef[:, s:s + 1], None, ALU.mult)
                                else:
                                    dve.wait_ge(sem("row_used"), s - 1)
                                    ins = nc.vector.scalar_tensor_tensor(out=into, in0=v_row, scalar=coef[:, s:s + 1],
                                                                         in1=into, op0=ALU.mult, op1=ALU.add)
                                ins.then_inc(sem("row_used"), 1)

                        chain(nc.vector.tensor_copy(cut(P_MEM, "sc"),
                                                    cut(P_MEM, "s12")[:, bass.ds(a * (2 * PH * NK), 2 * PH * NK)]))
                        chain(nc.vector.tensor_copy(ht_now, memT[:, bass.ds(a * D, D)]))
                        select(0)
                        for s in range(0, NSLOT + PAIR, PAIR):
                            if s < NSLOT:
                                if s % TOPK == 0 and s // TOPK + 1 < PH:
                                    select(s // TOPK + 1)
                                dots(s)
                            if s:
                                accumulate(s - PAIR)
                        dve.wait_ge(sem("row_used"), NSLOT)
                        nc.vector.tensor_tensor(memT[:, bass.ds(a * D, D)], acc[:, 0, :], acc[:, 1, :], ALU.add
                                                ).then_inc(sem("sum_made"), 1)
                        dve.wait_ge(sem("sum_made"), 1)
                clear_semaphores()

        def peer_out_pe(pe):
            for i in range(4):
                for j in range(2):
                    f = 2 * i + j
                    for a in range(TT):
                        ins = nc.tensor.transpose(T_[i][:, j * T + a * P:j * T + (a + 1) * P],
                                                  ht[:, a, f * P:(f + 1) * P], ident)
                ins.then_inc(sem("sum_turned"), 1)

        def peer_out_block(l):
            with nc.Block() as block:
                @block.tensor
                def _(pe):
                    peer_out_pe(pe)
                    norm_pe(pe, "lnp", lambda f: pe.wait_ge(sem("res_made"), f + 1), x3, KD)

                @block.scalar
                def _(act):
                    for f in range(KD):
                        act.wait_ge(sem("sum_turned"), f // 2 + 1)
                        nc.scalar.activation(sq[:, f, :], T_[f // 2][:, (f % 2) * T:(f % 2 + 1) * T], ACT.Copy,
                                             scale=mod_part(l, 5, f)).then_inc(sem("gated"), 1)
                    norm_act(act, "lnp", KD, x3, vb, POST, "g", "b", off=(2 * l + 1) * KD)

                @block.vector
                def _(dve):
                    gated_residual_dve(dve, lambda f: dve.wait_ge(sem("gated"), f + 1), "res_made")
                    norm_dve(dve, "lnp", x3, KD)

                if l == DEPTH - 1:
                    @block.sync
                    def _(sp):
                        sp.wait_ge(sem("lnp_out"), KD)
                        sp.dma_start(out, xT[:, :]).then_inc(sem("out_written"), 16)
                        sp.wait_ge(sem("out_written"), 16)
            if l < DEPTH - 1:
                clear_semaphores()

        peer(0)
        peer_out_block(0)

        PAD = max(WINDOWS) // 2
        W = T + 2 * PAD
        hc3 = cut(C_MEM, "pooled", "p (f t) -> p f t", f=KD)
        zp = cut(C_MEM, "zp", "p (f t) -> p f t", f=KD)
        s1 = cut(C_MEM, "s1", "p (f t) -> p f t", f=2)
        s2 = cut(C_MEM, "s2", "p (f t) -> p f t", f=2)
        yg = cut(C_MEM, "yg", "p (f t) -> p f t", f=KD)
        invcnt = cst[:, CONST["invcnt"]].rearrange("p (g t) -> p g t", g=GROUPS)

        with nc.Block() as block:
            @block.sync
            def _(sp):
                stream(sp, C_PANELS, C_TILES, DEPTH * len(A_PANELS) + len(B_PANELS), False)

            @block.gpsimd
            def _(pool):
                nc.gpsimd.memset(zp[:, :, 0:PAD], 0.0).then_inc(sem("pad_set"), 1)
                nc.gpsimd.memset(zp[:, :, PAD + T:], 0.0).then_inc(sem("pad_set"), 1)

            @block.tensor
            def _(pe):
                e = PE(pe, C_PANELS, C_TILES)
                rd = Reader(pe, C_TILES)
                pe.wait_ge(sem("h_made"), KD)
                for i in range(2):
                    e.feature_tiles(e.panel("pin", i), "pin", 4 * i, 4, KD, hc3, T)
                w = e.panel("grp", 0)
                for j in range(KD):
                    g = j // 2
                    pe.wait_ge(sem("pooled"), g + 1)
                    bank = e.bank("grp", j)
                    for k in range(2):
                        ins = nc.tensor.matmul(bank[:, 0:T], w[:, (2 * j + k) * P:(2 * j + k + 1) * P],
                                               hc3[:, 2 * g + k, :], start=(k == 0), stop=(k == 1))
                    e.filled(ins, "grp", j)
                for f in range(KD):
                    rd.read_wait("grp", f)
                for i in range(2):
                    e.feature_tiles(e.panel("pout", i), "pout", 4 * i, 4, KD, yg, T)
                norm_pe(pe, "lnc", lambda f: pe.wait_ge(sem("res_made"), f + 1), x3, KD)
                peer_prep_pe(e, rd)

            @block.scalar
            def _(act):
                rd = Reader(act, C_TILES)
                for f in range(KD):
                    nc.scalar.activation(hc3[:, f, :], x3[:, f, :], ACT.Identity, scale=mod_part(1, 1, f),
                                         bias=mod_part(1, 0, f)).then_inc(sem("h_made"), 1)
                for f in range(KD):
                    rd.free(nc.scalar.activation(zp[:, f, PAD:PAD + T], rd.full("pin", f)[:, 0:T], ACT.Copy), "pin", f)
                for f in range(KD):
                    rd.free(nc.scalar.activation(yg[:, f, :], rd.full("grp", f)[:, 0:T], ACT.Copy,
                                                 scale=vcol(vb, VEC_B, "pool_scale", f)), "grp", f)
                gated_act(act, rd, "pout", 1, 2)
                norm_act(act, "lnc", KD, x3, vb, POST, "g", "b", off=2 * KD)
                peer_prep_act(act, rd, 1, "lnc")

            @block.vector
            def _(dve):
                rd = Reader(dve, C_TILES)
                dve.wait_ge(sem("pad_set"), 2)
                for f in range(KD):
                    rd.full("pin", f)
                steps = 0
                for g, w in enumerate(WINDOWS):
                    for f in (2 * g, 2 * g + 1):
                        rd.read_wait("pin", f)
                    src, n, size = zp[:, 2 * g:2 * g + 2, :], W, 1
                    dst, other = s1, s2
                    while size < w:
                        n -= size
                        nc.vector.tensor_tensor(dst[:, :, 0:n], src[:, :, 0:n], src[:, :, size:size + n], ALU.add
                                                ).then_inc(sem("doubled"), 1)
                        steps += 1
                        dve.wait_ge(sem("doubled"), steps)
                        src, dst, other, size = dst, other, dst, 2 * size
                    at = PAD - w // 2
                    nc.vector.tensor_tensor(dst[:, :, 0:T], src[:, :, at:at + T],
                                            invcnt[:, g:g + 1, :].broadcast_to([P, 2, T]), ALU.mult
                                            ).then_inc(sem("doubled"), 1)
                    steps += 1
                    dve.wait_ge(sem("doubled"), steps)
                    nc.vector.tensor_tensor(hc3[:, 2 * g:2 * g + 2, :], dst[:, :, 0:T],
                                            zp[:, 2 * g:2 * g + 2, PAD:PAD + T], ALU.subtract
                                            ).then_inc(sem("pooled"), 1)
                    dve.wait_ge(sem("pooled"), g + 1)
                gated_residual_dve(dve, lambda f: rd.read_wait("pout", f), "res_made")
                norm_dve(dve, "lnc", x3, KD)
                peer_prep_dve(dve, rd)
        clear_semaphores()
        peer(1)
        peer_out_block(1)


def feature_major(x):
    t, d = x.shape
    return np.ascontiguousarray(x.T.reshape(d // P, P, t).transpose(1, 0, 2)).reshape(P, -1)


def by_partition(v):
    return np.moveaxis(v.reshape(*v.shape[:-1], -1, P), -1, 0).reshape(P, -1)


def feature_panel(w, tiles):
    k = w.shape[0] // P
    parts = [w[:, c].reshape(k, P, P).transpose(1, 0, 2).reshape(P, -1) for c in tiles]
    return pad(np.concatenate(parts, axis=1))


def token_panel(w):
    return pad(w.reshape(-1, P, w.shape[1]).transpose(1, 0, 2).reshape(P, -1))


def pad(w):
    return np.pad(w, ((0, 0), (0, PANEL - w.shape[1])))


def tile(i):
    return slice(i * P, (i + 1) * P)


def lay_out(a):
    panels = []
    cuts = np.cumsum([0, CONV, CONV, GH * GK, GH * GK, GH * GV, GH * GV, RANK])
    for l in range(DEPTH):
        w = a["w_in"][l]
        c_a, c_g, q, k, v, r, _ = (w[:, cuts[i]:cuts[i + 1]] for i in range(7))
        wi, wk, wm = a["w_ffn_in"][l], a["w_xkv"][l], a["w_mod_2"][l]
        made = {
            "glu": lambda i: feature_panel(np.concatenate([x[:, tile(j)] for j in (2 * i, 2 * i + 1) for x in (c_g, c_a)],
                                                          axis=1), [tile(j) for j in range(4)]),
            "qk": lambda i: feature_panel(np.concatenate([q, k], axis=1), [tile(j) for j in range(4)]),
            "v": lambda i: token_panel(v),
            "r": lambda i: feature_panel(r, [tile(j) for j in range(4)]),
            "xk": lambda i: feature_panel(wk, [tile(4 * i + j) for j in range(4)]),
            "xv": lambda i: token_panel(wk[:, D + 512 * i:D + 512 * (i + 1)]),
            "mod": lambda i: feature_panel(wm, [tile(4 * i + j) for j in range(4)]),
            "fi": lambda i: feature_panel(wi, [tile(c) for j in (2 * i, 2 * i + 1) for c in (j, KF + j)]),
            "fo": lambda i: feature_panel(a["w_ffn_out"][l], [tile(i)]),
            **{s: (lambda w: lambda i: feature_panel(w, [tile(4 * i + j) for j in range(4)]))(a[n][l])
               for s, n in (("mix", "w_mix_out"), ("xq", "w_xq"), ("xo", "w_xo"))},
        }
        panels += [made[s](i) for s, i in A_PANELS]
    wz, wu, wkv = a["mla_w_in_2"][0], a["mla_w_uq_2"][0], a["mla_w_ukv_2"][0]
    kr = wz[:, QL + KVL:]
    half = ROPE // 2
    wz = np.concatenate([wz[:, :QL + KVL]] + [kr[:, :half]] * 4 + [kr[:, half:]] * 4, axis=1)
    wu = wu.reshape(QL, MH, NOPE + ROPE)
    wu = np.concatenate([x.reshape(QL, -1) for x in (wu[:, :, :NOPE], wu[:, :, NOPE:NOPE + half],
                                                     wu[:, :, NOPE + half:])], axis=1)
    wkv = wkv.reshape(KVL, MH, NOPE + VD)
    four = lambda w: lambda i: feature_panel(w, [tile(4 * i + j) for j in range(4)])

    def peer(l):
        k12 = np.stack([a["peer_k1_2"][l], a["peer_k2_2"][l]], axis=1)
        return {"pq": four(a["peer_w_q_2"][l]), "pk": lambda i: pad(k12.transpose(3, 0, 1, 2).reshape(P, -1))}

    made = {
        "zi": lambda i: feature_panel(wz, [tile(j) for j in range(4 * i, min(4 * i + 4, 7))]),
        "uq": lambda i: feature_panel(wu, [tile(6 * i + j) for j in range(6)]),
        "ukv": lambda i: pad(np.concatenate([
            feature_panel(wkv[:, :, :NOPE].reshape(KVL, -1), [tile(j) for j in range(8)])[:, :2048],
            token_panel(wkv[:, :, NOPE:].reshape(KVL, -1))[:, :2048]], axis=1)),
        "wo": four(a["mla_w_o_2"][0]), **peer(0)}
    panels += [made[s](i) for s, i in B_PANELS]
    grp = a["pool_w_grp_2"][0]
    made = {
        "pin": four(a["pool_w_in_2"][0]), "pout": four(a["pool_w_out_2"][0]),
        "grp": lambda i: pad(np.concatenate([feature_panel(grp[j // 2], [tile(j % 2)])[:, :2 * P] for j in range(8)],
                                            axis=1)), **peer(1)}
    panels += [made[s](i) for s, i in C_PANELS]

    vec_a = np.stack([np.concatenate(
        [by_partition(a[n][l]) for n in ("ln1_g", "ln1_b", "ln2_g", "ln2_b", "ln3_g", "ln3_b")]
        + [a["conv_w"][l].T.reshape(CF, P, TAPS).transpose(1, 0, 2).reshape(P, -1)]
        + [by_partition(a[n][l]) for n in ("conv_b", "conv_ln_g", "conv_ln_b", "gla_norm_g", "b_a")]
        + [a["w_in"][l][:, cuts[6]:].reshape(KD, P, RANK).transpose(1, 0, 2).reshape(P, -1)]
        + [np.pad(a["w_a2"][l], ((0, P - RANK), (0, 0)))]
        + [by_partition(a["b_mod_2"][l])], axis=1) for l in range(DEPTH)])
    c2 = np.stack([a["c_2"][0], a["c_ctx_2"]])
    vec_b = np.concatenate([by_partition(a["ln0_g"]), by_partition(a["ln0_b"]),
                            c2.reshape(2, KD, P).transpose(2, 1, 0).reshape(P, -1),
                            by_partition(a["ln_g_2"]), by_partition(a["ln_b_2"]),
                            by_partition(a["mla_q_norm_2"][0]), by_partition(a["mla_kv_norm_2"][0]),
                            by_partition(a["pool_scale_2"][0])], axis=1)
    acts = np.stack([feature_major(a["x"][0]), feature_major(a["mem"][0]), feature_major(a["ctx_2"][0])])
    return {"panels": np.stack(panels), "vec_a": vec_a, "vec_b": vec_b, "consts": shape_constants(),
            "mask": causal_mask(), "acts": acts,
            "tables": np.concatenate([a["peer_u_2"], a["peer_v_2"]], axis=2).reshape(DEPTH * NEXP, 2 * D)}


def causal_mask():
    s, c = np.arange(P)[:, None], np.arange(P)[None, :]
    return ((s <= c) & (s // CHUNK == c // CHUNK)).astype(np.uint32)


def shape_constants():
    n_freq, grid = ROPE // 4, 64
    t = np.arange(T)
    freqs = (np.float32(10000.0) ** (-np.arange(n_freq, dtype=np.float32) / n_freq)).astype(np.float32)
    ang = np.concatenate([(t // grid).astype(np.float32)[:, None] * freqs,
                          (t % grid).astype(np.float32)[:, None] * freqs], axis=1).astype(np.float32)
    cos = np.concatenate([np.tile(np.cos(ang).T, (4, 1)), np.ones((P, T), np.float32)], axis=1)
    sin = np.concatenate([np.tile(np.sin(ang).T, (4, 1)), np.zeros((P, T), np.float32)], axis=1)
    scan = np.tile((t % CHUNK != 0).astype(np.float32), (P, 1))
    count = [np.clip(t + w // 2, 0, T) - np.clip(t - w // 2, 0, T) for w in WINDOWS]
    inv = np.tile((1.0 / np.concatenate(count)).astype(np.float32), (P, 1))
    iota = np.tile(np.arange(TOPK, dtype=np.float32), (P, 1))
    return np.concatenate([np.eye(P, dtype=np.float32), cos, sin, scan, iota, inv], axis=1).astype(np.float32)


def kernel(**inputs):
    import concourse.bacc as bacc
    from concourse.bass_utils import run_bass_kernel_spmd

    arrays = {n: np.ascontiguousarray(x) for n, x in lay_out({n: np.asarray(x) for n, x in inputs.items()}).items()}
    nc = bacc.Bacc("TRN2", target_bir_lowering=False, num_devices=1)
    aps = [nc.dram_tensor(n, x.shape, mybir.dt.from_np(x.dtype), kind="ExternalInput").ap() for n, x in arrays.items()]
    out = nc.dram_tensor("out", (P, KD * T), F32, kind="ExternalOutput").ap()
    build_program(nc, aps[0], aps[1], aps[2], aps[3], aps[4], aps[5], aps[6], out)
    got = run_bass_kernel_spmd(nc, [arrays], core_ids=[0]).results[0]["out"]
    return got.reshape(P, KD, T).transpose(2, 1, 0).reshape(1, T, D)
```

```python
from contextlib import ExitStack

import numpy as np

import concourse.bass as bass
from concourse import mybir

F32 = mybir.dt.float32
U32 = mybir.dt.uint32
ALU = mybir.AluOpType
ACT = mybir.ActivationFunctionType
AX_X = mybir.AxisListType.X

P = 128
D = 1024
KD = D // P
T = 256
TT = T // P
DEPTH = 2
ALPHA = (2 * DEPTH) ** 0.25
LN_EPS, RMS_EPS = 1e-5, 1e-6

CONV, TAPS = 512, 31
CF = CONV // P
GH, GK, GV, CHUNK = 4, 64, 128, 64
GF = GH * GK // P
NCHUNK = T // CHUNK
RANK = 16
XH = 4
FF = 2816
KF = FF // P

MH, NOPE, ROPE, VD = 8, 128, 64, 128
QL, KVL = 384, 256
GROUPS, WINDOWS = 4, (2, 4, 8, 16)
PH, NK, TOPK = 8, 128, 16
NEXP = NK * NK

PANEL = KD * 4 * P
SLOTS = 4
AHEAD = 2
NBANK = 4
NEG = -3.0e38


A_PANELS = [("glu", 0), ("glu", 1), ("qk", 0), ("v", 0), ("r", 0), ("xk", 0), ("xv", 0), ("xv", 1),
            ("mix", 0), ("mix", 1), ("xk", 1), ("xq", 0), ("mod", 0), ("xq", 1), ("xo", 0), ("xo", 1)]
for i in range(11):
    A_PANELS += [("fi", i)] + ([("mod", 1 + i)] if i < 8 else [])
for i in range(8):
    A_PANELS += [("fo", i)] + ([("mod", 9 + i // 2)] if i in (0, 2, 4) else [])
B_PANELS = ([("zi", 0), ("zi", 1), ("uq", 0), ("uq", 1), ("ukv", 0), ("wo", 0), ("wo", 1)]
            + [("pq", 0), ("pk", 0), ("pq", 1), ("pq", 2), ("pq", 3)])
C_PANELS = ([("pin", 0), ("pin", 1), ("grp", 0), ("pout", 0), ("pout", 1)]
            + [("pq", 0), ("pk", 0), ("pq", 1), ("pq", 2), ("pq", 3)])
NPANELS = DEPTH * len(A_PANELS) + len(B_PANELS) + len(C_PANELS)

A_TILES = ([("glu", i) for i in range(8)] + [("qk", i) for i in range(4)] + [("v", i) for i in range(2)]
           + [("r", i) for i in range(4)] + [("xk", i) for i in range(4)] + [("upd", i) for i in range(3)]
           + [("xv", i) for i in range(2)] + [("o", i) for i in range(4)] + [("xv", i) for i in range(2, 4)]
           + [("mix", i) for i in range(8)] + [("xk", 4), ("xk", 5)] + [("xq", i) for i in range(8)]
           + [("xk", 6), ("xk", 7)] + [("sc", i) for i in range(8)]
           + [("pt", i) for i in range(4)] + [("ox", i) for i in range(8)] + [("xo", i) for i in range(8)]
           + [("fi", i) for i in range(44)] + [("fo", i) for i in range(8)])
PEER_TILES = ([("pq", i) for i in range(4)] + [("ps", 0)] + [("pq", i) for i in range(4, 16)]
              + [("ht", i) for i in range(4)] + [("ps", i) for i in range(1, 8)])
B_TILES = ([("zi", i) for i in range(7)] + [("uq", i) for i in range(12)] + [("kn", i) for i in range(8)]
           + [("vm", i) for i in range(8)]
           + [t for h in range(MH) for t in [("sc", 2 * h), ("sc", 2 * h + 1)]
              + ([("pt", 2 * h - 2), ("pt", 2 * h - 1), ("ox", h - 1)] if h else [])]
           + [("pt", 14), ("pt", 15), ("ox", 7)] + [("wo", i) for i in range(8)] + PEER_TILES)
C_TILES = ([("pin", i) for i in range(8)] + [("grp", i) for i in range(8)] + [("pout", i) for i in range(8)]
           + PEER_TILES)


LAST_TILE = {("v", 0): ("v", 1), ("xv", 0): ("xv", 1), ("xv", 1): ("xv", 3), ("zi", 1): ("zi", 6), ("uq", 0): ("uq", 5),
             ("uq", 1): ("uq", 11), ("ukv", 0): ("vm", 7), ("grp", 0): ("grp", 7), ("pk", 0): ("ps", 7),
             **{("fo", i): ("fo", i) for i in range(8)}}


def columns(widths):
    at, out = 0, {}
    for name, w in widths:
        out[name] = slice(at, at + w)
        at += w
    return out, at


VEC_A, NVEC_A = columns([("ln1_g", 8), ("ln1_b", 8), ("ln2_g", 8), ("ln2_b", 8), ("ln3_g", 8), ("ln3_b", 8),
                         ("conv_w", CF * TAPS), ("conv_b", CF), ("cln_g", CF), ("cln_b", CF), ("gla_g", 1),
                         ("b_a", GF), ("w_low", KD * RANK), ("w_a2", GH * GK), ("b_mod", 48)])
VEC_B, NVEC_B = columns([("ln0_g", 8), ("ln0_b", 8), ("ln_g", 32), ("ln_b", 32),
                         ("q_norm", 3), ("kv_norm", 2), ("pool_scale", 8)])
CONST, NCONST = columns([("ident", P), ("cos", 2 * T), ("sin", 2 * T), ("scan", T), ("iota", TOPK),
                         ("invcnt", GROUPS * T)])

ARENA = 28928
LN_W = [("xc", KD * T), ("sq", KD * T), ("sd", T), ("rstd", T)]
A_MEM, A_END = columns(LN_W + [
    ("xk", KD * T), ("xv", TT * D), ("mix", KD * T),
    ("glu", CF * (TAPS - 1 + T)), ("sig", 4 * T), ("cy", CF * T), ("q", GF * T), ("k", GF * T), ("r", CF * T),
    ("v", TT * GH * GV), ("low", T), ("z", GF * T), ("za", GF * T), ("bc", GF * T), ("ep", GF * T),
    ("en", GF * T), ("qe", GF * T), ("ke", GF * T), ("kd", GF * T),
    ("kdt", TT * GH * GK), ("att", 8 * P), ("st", 3 * GF * GV), ("o", GH * T), ("rs", GH * T),
    ("cs", 2 * D), ("junk", D)])
A_MEM["ed"] = A_MEM["za"]
A_SHARE = A_MEM["glu"].start
X_MEM, X_END = columns([("pad", A_SHARE), ("qx", KD * T), ("p", 8 * T), ("pt", XH * TT * T), ("ox", KD * T)])
F_MEM, F_END = columns([("pad", A_SHARE), ("sg", 4 * T), ("hid", KF * T)])
B_MEM, B_END = columns(LN_W + [
    ("h", KD * 2 * T), ("cq", 3 * T), ("ckv", 2 * 2 * T), ("kr", 2 * 2 * T), ("kro", 2 * 2 * T),
    ("qr", 4 * T), ("qro", 4 * T), ("qn", MH * T), ("kn", MH * 2 * T), ("vm", 4 * D), ("tmp", 2 * 2 * T),
    ("p", 2 * 2 * T), ("pt", 2 * 4 * P)])
B_OX = B_MEM["h"].start
C_MEM, C_END = columns(LN_W + [("zp", KD * (T + 16)), ("s1", 2 * (T + 16)), ("s2", 2 * (T + 16)),
                               ("pooled", KD * T), ("yg", KD * T)])
RING = 8
NDIAG = 4
PAIR = 2
P_MEM, P_END = columns([
    ("ring", RING * 2 * D), ("s12", TT * 2 * PH * NK), ("wk", 2 * NK),
    ("v16", 2 * TOPK), ("i16", 2 * TOPK), ("if", 2 * TOPK), ("cand", T), ("cw", T), ("top", TOPK), ("pos", TOPK),
    ("ab", 2 * TOPK), ("abf", 2 * TOPK), ("oh", T), ("sel", 2 * TOPK), ("idf", TOPK), ("idx", 2 * TOPK),
    ("gate", 2 * TOPK), ("gs", 4), ("dot", 2 * TOPK), ("act", 2 * TOPK),
    ("diag", NDIAG * P)])
Q_MEM, Q_END = columns([("pad", P_END), ("hp", KD * T), ("pq", 16 * T)])
assert max(A_END, X_END, F_END, B_END, C_END, P_END, Q_END) <= ARENA


class Ring:

    def __init__(self, tiles):
        self.order = {t: n for n, t in enumerate(tiles)}
        assert len(self.order) == len(tiles)

    def at(self, stage, i):
        n = self.order[(stage, i)]
        return n % NBANK, n // NBANK


def build_program(nc, panels, vec_a, vec_b, consts, mask_in, acts, tables, c_rows, out):
    with ExitStack() as ctx:
        def sb(name, cols, dt=F32):
            return ctx.enter_context(nc.sbuf_tensor(name, [P, cols], dt))

        sems = {}

        def sem(name):
            if name not in sems:
                sems[name] = ctx.enter_context(nc.semaphore(name))
            return sems[name]

        ring = sb("weight_ring", SLOTS * PANEL)
        xT = sb("xT", KD * T)
        memT = sb("memT", KD * T)
        ones = sb("ones", P)
        cst = sb("cst", NCONST)
        mask = sb("causal_mask", P, U32)
        va = sb("va", NVEC_A)
        vb = sb("vb", NVEC_B)
        eps = sb("eps", 2)
        modT = sb("modT", DEPTH * 96)
        small = sb("small", 144)
        mod_sum = small[:, 48:144].rearrange("p (j c) -> p j c", c=2)
        arena = sb("arena", ARENA)
        T_ = [ctx.enter_context(nc.psum_tensor(f"tile{b}", [P, 512], F32)) for b in range(NBANK)]
        M = [ctx.enter_context(nc.psum_tensor(f"misc{b}", [P, 512], F32)) for b in range(4)]

        def cut(mem, name, pat=None, **kw):
            ap = arena[:, mem[name]]
            return ap.rearrange(pat, **kw) if pat else ap

        x3 = xT[:, :].rearrange("p (f t) -> p f t", f=KD)
        mem3 = memT[:, :].rearrange("p (f t) -> p f t", f=KD)
        cond = cut(A_MEM, "cs", "p (c n) -> p c n", c=2)
        ident = cst[:, CONST["ident"]]
        mod4 = modT[:, :].rearrange("p (l j c) -> p l j c", l=DEPTH, c=2)
        xc = cut(A_MEM, "xc", "p (f t) -> p f t", f=KD)
        sq = cut(A_MEM, "sq", "p (f t) -> p f t", f=KD)
        sd, rstd = cut(A_MEM, "sd"), cut(A_MEM, "rstd")

        def vcol(tensor, table, name, i=0):
            c = table[name].start + i
            return tensor[:, c:c + 1]

        def panels_landed(n):
            return 16 * (n // SLOTS + (n % SLOTS >= AHEAD))

        class PE:

            def __init__(self, pe, panel_list, tiles):
                self.pe, self.list, self.n, self.tiles = pe, panel_list, 0, Ring(tiles)

            def panel(self, stage, i):
                while self.list[self.n][0] == "mod":
                    self.n += 1
                assert self.list[self.n] == (stage, i), (self.list[self.n], stage, i)
                n, self.n = self.n, self.n + 1
                if n >= AHEAD:
                    self.pe.wait_ge(sem(f"panel_landed{n % SLOTS}"), panels_landed(n))
                return ring[:, (n % SLOTS) * PANEL:(n % SLOTS + 1) * PANEL]

            def bank(self, stage, i):
                b, use = self.tiles.at(stage, i)
                if use:
                    self.pe.wait_ge(sem(f"bank_read{b}"), use)
                return T_[b]

            def filled(self, ins, stage, i):
                ins.then_inc(sem(f"bank_filled{self.tiles.at(stage, i)[0]}"), 1)

            def feature_tiles(self, w, stage, first, count, K, rhs, N, ready=None):
                for j in range(count):
                    bank = self.bank(stage, first + j)
                    for k in range(K):
                        c = (j * K + k) * P
                        if ready and j == 0:
                            ready(k)
                        ins = nc.tensor.matmul(bank[:, 0:N], w[:, c:c + P], rhs[:, k, 0:N],
                                               start=(k == 0), stop=(k == K - 1))
                    self.filled(ins, stage, first + j)

            def token_tiles(self, w, stage, first, count, K, lhs, width=512, off=0, start=0):
                for j in range(start, count):
                    bank = self.bank(stage, first + j)
                    for k in range(K):
                        ins = nc.tensor.matmul(bank[:, :], lhs[:, k, j * P:(j + 1) * P],
                                               w[:, off + k * width:off + k * width + 512],
                                               start=(k == 0), stop=(k == K - 1))
                    self.filled(ins, stage, first + j)

        def stat_pe(wait_written, signal, src, n, bank):
            for f in range(n):
                wait_written(f)
                ins = nc.tensor.matmul(bank, ones[:, :], src[:, f, :], start=(f == 0), stop=(f == n - 1))
            ins.then_inc(sem(signal), 1)

        def norm_pe(pe, ln, wait_written, src, n, between=None):
            stat_pe(wait_written, f"{ln}_sum", src, n, M[0][:, 0:T])
            if between:
                between()
            stat_pe(lambda f: pe.wait_ge(sem(f"{ln}_sq"), f + 1), f"{ln}_var", sq, n, M[3][:, T:2 * T])

        def norm_dve(dve, ln, src, n):
            dve.wait_ge(sem(f"{ln}_sum"), 1)
            for f in range(n):
                nc.vector.scalar_tensor_tensor(out=xc[:, f, :], in0=M[0][:, 0:T], scalar=-1.0 / (n * P),
                                               in1=src[:, f, :], op0=ALU.mult, op1=ALU.add
                                               ).then_inc(sem(f"{ln}_centred"), 1)
            dve.wait_ge(sem(f"{ln}_sd"), 1)
            nc.vector.reciprocal(rstd, sd).then_inc(sem(f"{ln}_rstd"), 1)
            dve.wait_ge(sem(f"{ln}_rstd"), 1)
            dve.wait_ge(sem(f"{ln}_centred"), n)
            for f in range(n):
                nc.vector.tensor_tensor(xc[:, f, :], xc[:, f, :], rstd, ALU.mult
                                        ).then_inc(sem(f"{ln}_scaled"), 1)

        def norm_act(act, ln, n, dst, tensor, table, g, b, off=0, func=ACT.Identity, between=None):
            for f in range(n):
                act.wait_ge(sem(f"{ln}_centred"), f + 1)
                nc.scalar.activation(sq[:, f, :], xc[:, f, :], ACT.Square).then_inc(sem(f"{ln}_sq"), 1)
            if between:
                between()
            act.wait_ge(sem(f"{ln}_var"), 1)
            nc.scalar.activation(sd, M[3][:, T:2 * T], ACT.Sqrt, scale=1.0 / (n * P), bias=eps[:, 0:1]
                                 ).then_inc(sem(f"{ln}_sd"), 1)
            for f in range(n):
                act.wait_ge(sem(f"{ln}_scaled"), f + 1)
                nc.scalar.activation(dst[:, f, :], xc[:, f, :], func, scale=vcol(tensor, table, g, off + f),
                                     bias=vcol(tensor, table, b, off + f)).then_inc(sem(f"{ln}_out"), 1)

        class Reader:

            def __init__(self, eng, tiles):
                self.eng, self.tiles = eng, Ring(tiles)

            def full(self, stage, i):
                b, use = self.tiles.at(stage, i)
                self.eng.wait_ge(sem(f"bank_filled{b}"), use + 1)
                return T_[b]

            def free(self, ins, stage, i):
                ins.then_inc(sem(f"bank_read{self.tiles.at(stage, i)[0]}"), 1)

            def read_wait(self, stage, i):
                b, use = self.tiles.at(stage, i)
                self.eng.wait_ge(sem(f"bank_read{b}"), use + 1)

        def stream(sp, panel_list, tiles, base, following, beside=None):
            rd, n = Reader(sp, tiles), len(panel_list)

            def wait_used(stage, i):
                if stage == "mod":
                    sp.wait_ge(sem("mod_summed"), i + 1)
                else:
                    rd.full(*LAST_TILE.get((stage, i), (stage, 4 * i + 3)))

            def load(j, slot, landed):
                sp.dma_start(ring[:, slot * PANEL:(slot + 1) * PANEL],
                             panels[bass.ds(base + j, 1)].rearrange("a p c -> (a p) c")).then_inc(sem(landed), 16)

            for j in range(AHEAD, n):
                if j >= SLOTS:
                    wait_used(*panel_list[j - SLOTS])
                load(j, j % SLOTS, f"panel_landed{j % SLOTS}")
                if beside and j == SLOTS - 1:
                    beside()
            if following:
                for j in range(AHEAD):
                    wait_used(*panel_list[max(i for i in range(n) if i % SLOTS == j)])
                    load(n + j, j, "next_landed")
                sp.wait_ge(sem("next_landed"), 16 * AHEAD)

        def first_panels(sp, base):
            for j in range(AHEAD):
                sp.dma_start(ring[:, j * PANEL:(j + 1) * PANEL], panels[base + j]).then_inc(sem("next_landed"), 16)
            sp.wait_ge(sem("next_landed"), 16 * AHEAD)

        def clear_semaphores():
            names = [name for name in sems if not name.startswith("row_landed")]

            def clear(eng, part):
                for name in names[part::4]:
                    eng.sem_clear(sems[name])

            with nc.Block() as block:
                @block.sync
                def _(sp):
                    clear(sp, 0)

                @block.gpsimd
                def _(pool):
                    clear(pool, 1)

                @block.vector
                def _(dve):
                    clear(dve, 2)

                @block.scalar
                def _(act):
                    clear(act, 3)

        with nc.Block() as block:
            @block.sync
            def _(sp):
                sp.dma_start(xT[:, :], acts[0]).then_inc(sem("x_landed"), 16)
                sp.dma_start(vb[:, :], vec_b).then_inc(sem("vec_landed"), 16)
                first_panels(sp, 0)

            @block.gpsimd
            def _(pool):
                nc.gpsimd.memset(ones[:, :], 1.0).then_inc(sem("ones_set"), 1)
                nc.gpsimd.memset(eps[:, 0:1], LN_EPS).then_inc(sem("eps_set"), 1)
                nc.gpsimd.memset(eps[:, 1:2], RMS_EPS).then_inc(sem("eps_set"), 1)
                nc.gpsimd.memset(small[:, 48:144], 0.0)

            @block.tensor
            def _(pe):
                pe.wait_ge(sem("ones_set"), 1)
                pe.wait_ge(sem("x_landed"), 16)
                for f in range(KD):
                    ins = nc.tensor.matmul(M[0][:, 0:T], ones[:, :], x3[:, f, :], start=(f == 0), stop=(f == KD - 1))
                ins.then_inc(sem("ln0_sum"), 1)
                stat_pe(lambda f: pe.wait_ge(sem("ln0_sq"), f + 1), "ln0_var", sq, KD, M[3][:, T:2 * T])

            @block.vector
            def _(dve):
                dve.wait_ge(sem("x_landed"), 16)
                norm_dve(dve, "ln0", x3, KD)

            @block.scalar
            def _(act):
                act.wait_ge(sem("vec_landed"), 16)
                act.wait_ge(sem("eps_set"), 2)
                norm_act(act, "ln0", KD, x3, vb, VEC_B, "ln0_g", "ln0_b")
        clear_semaphores()

        glu = cut(A_MEM, "glu", "p (f t) -> p f t", f=CF)
        sig = cut(A_MEM, "sig", "p (f t) -> p f t", f=4)
        cy = cut(A_MEM, "cy", "p (f t) -> p f t", f=CF)
        mix = cut(A_MEM, "mix", "p (f t) -> p f t", f=KD)
        gq, gk = (cut(A_MEM, n, "p (f t) -> p f t", f=GF) for n in ("q", "k"))
        r = cut(A_MEM, "r", "p (f t) -> p f t", f=CF)
        v = cut(A_MEM, "v", "p (a n) -> p a n", a=TT)
        low = cut(A_MEM, "low")
        flat = {n: cut(A_MEM, n) for n in ("z", "za", "bc", "ep", "en", "ed", "qe", "ke", "kd", "q", "k")}
        gf = {n: cut(A_MEM, n, "p (f t) -> p f t", f=GF) for n in ("z", "za", "bc", "ep", "en", "ed", "qe", "ke", "kd")}
        kdt = cut(A_MEM, "kdt", "p (a n) -> p a n", a=TT)
        att = cut(A_MEM, "att", "p (a n) -> p a n", a=8)
        st = cut(A_MEM, "st", "p (c f n) -> p c f n", c=3, f=GF)
        o = cut(A_MEM, "o", "p (h t) -> p h t", h=GH)
        rs = cut(A_MEM, "rs", "p (h t) -> p h t", h=GH)
        xk = cut(A_MEM, "xk", "p (f t) -> p f t", f=KD)
        xv = cut(A_MEM, "xv", "p (a n) -> p a n", a=TT)
        qx = cut(X_MEM, "qx", "p (f t) -> p f t", f=KD)
        px = cut(X_MEM, "p", "p (a t) -> p a t", a=8)
        ptx = cut(X_MEM, "pt", "p (h m t) -> p h m t", h=XH, m=TT)
        oxx = cut(X_MEM, "ox", "p (f t) -> p f t", f=KD)
        sg = cut(F_MEM, "sg", "p (f t) -> p f t", f=4)
        hid = cut(F_MEM, "hid", "p (f t) -> p f t", f=KF)
        nmax, rsum, rinv = small[:, 0:16], small[:, 16:32], small[:, 32:48]
        conv_w = va[:, VEC_A["conv_w"]].rearrange("p (f j) -> p f j", f=CF)
        w_low = va[:, VEC_A["w_low"]].rearrange("p (k n) -> p k n", k=KD)
        w_a2 = va[0:RANK, VEC_A["w_a2"]]

        with nc.Fori(0, DEPTH) as layer:
            with nc.Block() as block:
                @block.sync
                def _(sp):
                    sp.dma_start(va[:, :], vec_a[bass.ds(layer, 1)].rearrange("a p c -> (a p) c")
                                 ).then_inc(sem("vec_landed"), 16)
                    sp.dma_start(cst[:, :], consts).then_inc(sem("const_landed"), 16)
                    sp.dma_start(mask[:, :], mask_in).then_inc(sem("const_landed"), 16)

                    def memory_and_conditions():
                        sp.dma_start(memT[:, :], acts[1]).then_inc(sem("mem_landed"), 16)
                        sp.dma_start(cut(A_MEM, "cs"), c_rows).then_inc(sem("c_landed"), 16)

                    stream(sp, A_PANELS, A_TILES, layer * len(A_PANELS), True, memory_and_conditions)

                @block.tensor
                def _(pe):
                    e = PE(pe, A_PANELS, A_TILES)
                    rd = Reader(pe, A_TILES)

                    def full_panel(stage, i, rhs, ready=None):
                        e.feature_tiles(e.panel(stage, i), stage, 4 * i, 4, KD, rhs, T, ready)

                    full_panel("glu", 0, x3)
                    full_panel("glu", 1, x3)
                    pe.wait_ge(sem("vec_landed"), 16)
                    for k in range(KD):
                        ins = nc.tensor.matmul(M[0][0:RANK, 0:T], w_low[:, k, :], x3[:, k, :],
                                               start=(k == 0), stop=(k == KD - 1))
                    ins.then_inc(sem("low_filled"), 1)
                    full_panel("qk", 0, x3)
                    pe.wait_ge(sem("low_read"), 1)
                    for f in range(GF):
                        ins = nc.tensor.matmul(M[1][:, f * T:(f + 1) * T], w_a2[:, f * P:(f + 1) * P],
                                               low[0:RANK, :], start=True, stop=True)
                    ins.then_inc(sem("z_filled"), 1)
                    e.token_tiles(e.panel("v", 0), "v", 0, TT, KD, x3)
                    full_panel("r", 0, x3)
                    pe.wait_ge(sem("mem_landed"), 16)
                    full_panel("xk", 0, mem3)
                    pe.wait_ge(sem("const_landed"), 32)
                    pe.wait_ge(sem("kd_made"), 1)
                    for a in range(TT):
                        for f in range(GF):
                            c = (a * GF + f) * P
                            ins = nc.tensor.transpose(M[2][:, c:c + P], gf["kd"][:, f, a * P:(a + 1) * P], ident)
                    ins.then_inc(sem("kdt_filled"), 1)
                    pe.wait_ge(sem("qe_made"), 2)
                    for h in (0, 2, 1, 3):
                        rows = slice((h % 2) * GK, (h % 2 + 1) * GK)
                        for a in range(TT):
                            n = (h // 2) * TT + a
                            ins = nc.tensor.matmul(M[h % 2][:, n * P:(n + 1) * P],
                                                   gf["ke"][rows, h // 2, a * P:(a + 1) * P],
                                                   gf["qe"][rows, h // 2, a * P:(a + 1) * P], start=True, stop=True)
                        if h >= 2:
                            ins.then_inc(sem("att_filled"), 1)
                    pe.wait_ge(sem("kdt_read"), 1)
                    rd.read_wait("v", 0)
                    rd.read_wait("v", 1)
                    for c in range(NCHUNK - 1):
                        bank = e.bank("upd", c)
                        rows = slice((c % 2) * CHUNK, (c % 2 + 1) * CHUNK)
                        for h in range(GH):
                            cols = slice((h // 2) * GV, (h // 2 + 1) * GV)
                            ins = nc.tensor.matmul(bank[(h % 2) * GK:(h % 2 + 1) * GK, cols],
                                                   kdt[rows, c // 2, h * GK:(h + 1) * GK],
                                                   v[rows, c // 2, h * GV:(h + 1) * GV], start=True, stop=True)
                        e.filled(ins, "upd", c)
                    pe.wait_ge(sem("att_masked"), 8)
                    norm_pe(pe, "cln", lambda f: pe.wait_ge(sem("conv_made"), f + 1), cy, CF,
                            lambda: e.token_tiles(e.panel("xv", 0), "xv", 0, TT, KD, mem3))
                    for c in range(NCHUNK - 1):
                        rd.read_wait("upd", c)
                    pe.wait_ge(sem("state_half"), 2)
                    for h in range(GH):
                        bank = e.bank("o", h)
                        rows = slice((h % 2) * GK, (h % 2 + 1) * GK)
                        for a in range(TT):
                            nc.tensor.matmul(bank[:, a * P:(a + 1) * P], v[:, a, h * GV:(h + 1) * GV],
                                             att[:, (h % 2) * 4 + (h // 2) * TT + a, :], start=True, stop=False)
                            for c in range(max(1, 2 * a), 2 * a + 2):
                                ins = nc.tensor.matmul(bank[:, c * CHUNK:(c + 1) * CHUNK],
                                                       st[rows, c - 1, h // 2, :],
                                                       gf["qe"][rows, h // 2, c * CHUNK:(c + 1) * CHUNK],
                                                       start=False, stop=(c == 2 * a + 1))
                        e.filled(ins, "o", h)
                    xv1 = e.panel("xv", 1)
                    e.token_tiles(xv1, "xv", 2, 1, KD, mem3)
                    for h in range(GH):
                        pe.wait_ge(sem("osq_made"), h + 1)
                        nc.tensor.matmul(M[1 + h // 2][:, (h % 2) * T:(h % 2 + 1) * T], ones[:, :], sq[:, 4 + h, :],
                                         start=True, stop=True).then_inc(sem("rms_filled"), 1)
                    e.token_tiles(xv1, "xv", 2, 2, KD, mem3, start=1)

                    def mixed(k):
                        pe.wait_ge(sem("cln_out" if k < CF else "gated"), k % CF + 1)

                    full_panel("mix", 0, mix, mixed)
                    full_panel("mix", 1, mix)
                    xk1 = e.panel("xk", 1)
                    norm_pe(pe, "ln1", lambda f: rd.read_wait("mix", f), x3, KD,
                            lambda: e.feature_tiles(xk1, "xk", 4, 1, KD, mem3, T))
                    e.feature_tiles(xk1[:, KD * P:], "xk", 5, 1, KD, mem3, T)
                    full_panel("xq", 0, x3, lambda k: pe.wait_ge(sem("ln1_out"), k + 1))
                    full_panel("xq", 1, x3)
                    e.feature_tiles(xk1[:, 2 * KD * P:], "xk", 6, 2, KD, mem3, T)
                    for h in range(XH):
                        for k in range(2):
                            rd.read_wait("xq", 2 * h + k)
                            rd.read_wait("xk", 2 * h + k)
                        for a in range(TT):
                            bank = e.bank("sc", h * TT + a)
                            for k in range(2):
                                ins = nc.tensor.matmul(bank[:, 0:T], qx[:, 2 * h + k, a * P:(a + 1) * P],
                                                       xk[:, 2 * h + k, :], start=(k == 0), stop=(k == 1))
                            e.filled(ins, "sc", h * TT + a)
                    for h in range(XH):
                        pe.wait_ge(sem("px_made"), TT * (h + 1))
                        bank = e.bank("pt", h)
                        for m in range(TT):
                            for a in range(TT):
                                ins = nc.tensor.transpose(bank[:, m * T + a * P:m * T + (a + 1) * P],
                                                          px[:, h * TT + a, m * P:(m + 1) * P], ident)
                        e.filled(ins, "pt", h)
                    for i in range(4):
                        rd.read_wait("xv", i)
                    for f in range(KD):
                        rd.read_wait("pt", f // 2)
                        bank = e.bank("ox", f)
                        for m in range(TT):
                            ins = nc.tensor.matmul(bank[:, 0:T], xv[:, m, f * P:(f + 1) * P], ptx[:, f // 2, m, :],
                                                   start=(m == 0), stop=(m == TT - 1))
                        e.filled(ins, "ox", f)
                    full_panel("xo", 0, oxx, lambda k: rd.read_wait("ox", k))
                    full_panel("xo", 1, oxx)
                    norm_pe(pe, "ln2", lambda f: rd.read_wait("xo", f), x3, KD)
                    for i in range(11):
                        full_panel("fi", i, x3, None if i else lambda k: pe.wait_ge(sem("ln2_out"), k + 1))
                    for i in range(KD):
                        w = e.panel("fo", i)
                        bank = e.bank("fo", i)
                        for k in range(KF):
                            if i == 0:
                                rd.read_wait("fi", 2 * k + 1)
                            ins = nc.tensor.matmul(bank[:, 0:T], w[:, k * P:(k + 1) * P], hid[:, k, :],
                                                   start=(k == 0), stop=(k == KF - 1))
                        e.filled(ins, "fo", i)
                    norm_pe(pe, "ln3", lambda f: rd.read_wait("fo", f), x3, KD)

                @block.scalar
                def _(act):
                    rd = Reader(act, A_TILES)
                    for i in range(CF):
                        ins = nc.scalar.activation(sig[:, i, :], rd.full("glu", 2 * i)[:, 0:T], ACT.Sigmoid)
                        rd.free(ins, "glu", 2 * i)
                    act.wait_ge(sem("low_filled"), 1)
                    nc.scalar.activation(low[0:RANK, :], M[0][0:RANK, 0:T], ACT.Copy).then_inc(sem("low_read"), 1)
                    for i in range(4):
                        dst = (gq if i < GF else gk)[:, i % GF, :]
                        ins = nc.scalar.activation(dst, rd.full("qk", i)[:, 0:T], ACT.Copy,
                                                   scale=GK ** -0.5 if i < GF else 1.0)
                        rd.free(ins, "qk", i)
                    act.wait_ge(sem("vec_landed"), 16)
                    act.wait_ge(sem("z_filled"), 1)
                    for f in range(GF):
                        nc.scalar.activation(gf["z"][:, f, :], M[1][:, f * T:(f + 1) * T], ACT.Identity,
                                             bias=vcol(va, VEC_A, "b_a", f)).then_inc(sem("z_made"), 1)
                    act.wait_ge(sem("z_made"), GF)
                    nc.scalar.activation(flat["za"], flat["z"], ACT.Abs).then_inc(sem("act_gate"), 1)
                    act.wait_ge(sem("act_gate"), 1)
                    nc.scalar.activation(flat["za"], flat["za"], ACT.Exp, scale=-1.0).then_inc(sem("act_gate"), 1)
                    act.wait_ge(sem("act_gate"), 2)
                    nc.scalar.activation(flat["za"], flat["za"], ACT.Ln, bias=1.0).then_inc(sem("act_gate"), 1)
                    for i in range(TT):
                        ins = nc.scalar.activation(v[:, i, :], rd.full("v", i)[:, :], ACT.Copy)
                        rd.free(ins, "v", i)
                    act.wait_ge(sem("bc_made"), GF)
                    nc.scalar.activation(flat["ep"], flat["bc"], ACT.Exp, scale=1.0 / 16.0).then_inc(sem("ep_made"), 1)
                    nc.scalar.activation(flat["en"], flat["bc"], ACT.Exp, scale=-1.0 / 16.0).then_inc(sem("en_made"), 1)
                    act.wait_ge(sem("bd_made"), GF)
                    nc.scalar.activation(flat["ed"], flat["ed"], ACT.Exp, scale=1.0 / 16.0).then_inc(sem("ed_made"), 1)
                    for i in range(CF):
                        ins = nc.scalar.activation(r[:, i, :], rd.full("r", i)[:, 0:T], ACT.Silu)
                        rd.free(ins, "r", i)
                    for i in range(4):
                        ins = nc.scalar.activation(xk[:, i, :], rd.full("xk", i)[:, 0:T], ACT.Copy)
                        rd.free(ins, "xk", i)
                    act.wait_ge(sem("c_landed"), 16)
                    nc.scalar.activation(cut(A_MEM, "cs"), cut(A_MEM, "cs"), ACT.Silu).then_inc(sem("c_ready"), 1)
                    act.wait_ge(sem("kdt_filled"), 1)
                    nc.scalar.activation(cut(A_MEM, "kdt"), M[2][:, :], ACT.Copy).then_inc(sem("kdt_read"), 1)
                    def keys(first, count):
                        for i in range(first, first + count):
                            ins = nc.scalar.activation(xk[:, i, :], rd.full("xk", i)[:, 0:T], ACT.Copy)
                            rd.free(ins, "xk", i)

                    def values(first, count):
                        for i in range(first, first + count):
                            ins = nc.scalar.activation(xv[:, i % 2, (i // 2) * 512:(i // 2 + 1) * 512],
                                                       rd.full("xv", i)[:, :], ACT.Copy)
                            rd.free(ins, "xv", i)

                    norm_act(act, "cln", CF, mix, va, VEC_A, "cln_g", "cln_b", func=ACT.Silu,
                             between=lambda: values(0, 2))
                    for h in range(GH):
                        bank = rd.full("o", h)
                        nc.scalar.activation(sq[:, 4 + h, :], bank[:, 0:T], ACT.Square).then_inc(sem("osq_made"), 1)
                        ins = nc.scalar.activation(o[:, h, :], bank[:, 0:T], ACT.Copy)
                        rd.free(ins, "o", h)
                    values(2, 1)
                    for p in range(2):
                        act.wait_ge(sem("rms_filled"), 2 * p + 2)
                        nc.scalar.activation(rs[:, 2 * p:2 * p + 2, :].rearrange("p h t -> p (h t)"), M[1 + p][:, :],
                                             ACT.Sqrt, scale=1.0 / GV, bias=eps[:, 0:1]).then_inc(sem("rms_sd"), 1)
                    values(3, 1)
                    norm_act(act, "ln1", KD, x3, va, VEC_A, "ln1_g", "ln1_b", between=lambda: keys(4, 1))
                    keys(5, 1)
                    for i in range(KD):
                        ins = nc.scalar.activation(qx[:, i, :], rd.full("xq", i)[:, 0:T], ACT.Copy,
                                                   scale=(D // XH) ** -0.5)
                        rd.free(ins, "xq", i)
                    keys(6, 2)
                    for i in range(8):
                        bank = rd.full("sc", i)
                        act.wait_ge(sem("nmax_made"), i + 1)
                        ins = nc.scalar.activation(px[:, i, :], bank[:, 0:T], ACT.Exp, bias=nmax[:, i:i + 1],
                                                   accum_out=rsum[:, i:i + 1])
                        rd.free(ins, "sc", i)
                    for h in range(XH):
                        ins = nc.scalar.activation(ptx[:, h, :, :].rearrange("p m t -> p (m t)"),
                                                   rd.full("pt", h)[:, :], ACT.Copy)
                        rd.free(ins, "pt", h)
                    norm_act(act, "ln2", KD, x3, va, VEC_A, "ln2_g", "ln2_b")
                    for i in range(KF):
                        if i >= 4:
                            rd.read_wait("fi", 2 * i - 7)
                        ins = nc.scalar.activation(sg[:, i % 4, :], rd.full("fi", 2 * i)[:, 0:T], ACT.Silu)
                        rd.free(ins, "fi", 2 * i)
                    norm_act(act, "ln3", KD, x3, va, VEC_A, "ln3_g", "ln3_b")

                @block.gpsimd
                def _(pool):
                    nc.gpsimd.memset(glu[:, :, 0:TAPS - 1], 0.0).then_inc(sem("pad_set"), 1)
                    nc.gpsimd.memset(cut(A_MEM, "att"), 0.0).then_inc(sem("att_zeroed"), 1)
                    rd = Reader(pool, A_TILES)
                    for i in range(4):
                        rd.read_wait("qk", i)
                    pool.wait_ge(sem("ed_made"), 1)
                    nc.gpsimd.tensor_tensor(flat["kd"], flat["k"], flat["ed"], ALU.mult).then_inc(sem("kd_made"), 1)
                    nc.gpsimd.tensor_tensor(flat["qe"], flat["q"], flat["ep"], ALU.mult).then_inc(sem("qe_made"), 1)
                    nc.gpsimd.tensor_tensor(flat["ke"], flat["k"], flat["en"], ALU.mult).then_inc(sem("qe_made"), 1)

                @block.vector
                def _(dve):
                    rd = Reader(dve, A_TILES)
                    conv_steps = 0

                    def glu_tile(i):
                        rd.read_wait("glu", 2 * i)
                        ins = nc.vector.tensor_tensor(glu[:, i, TAPS - 1:], rd.full("glu", 2 * i + 1)[:, 0:T],
                                                      sig[:, i, :], ALU.mult)
                        rd.free(ins, "glu", 2 * i + 1)

                    def conv_pair(f0):
                        nonlocal conv_steps
                        for i in (f0, f0 + 1):
                            rd.read_wait("glu", 2 * i + 1)
                        for j in range(TAPS):
                            for i in (f0, f0 + 1):
                                if j == 0:
                                    ins = nc.vector.tensor_scalar(cy[:, i, :], glu[:, i, 0:T], conv_w[:, i, 0:1],
                                                                  vcol(va, VEC_A, "conv_b", i), ALU.mult, ALU.add)
                                else:
                                    dve.wait_ge(sem("tap_added"), conv_steps - 1)
                                    ins = nc.vector.scalar_tensor_tensor(
                                        out=cy[:, i, :], in0=glu[:, i, j:j + T], scalar=conv_w[:, i, j:j + 1],
                                        in1=cy[:, i, :], op0=ALU.mult, op1=ALU.add)
                                conv_steps += 1
                                if j == TAPS - 1:
                                    ins.then_inc(sem("conv_made"), 1)
                                else:
                                    ins.then_inc(sem("tap_added"), 1)
                        conv_steps -= 2

                    dve.wait_ge(sem("vec_landed"), 16)
                    dve.wait_ge(sem("pad_set"), 1)
                    for i in range(CF):
                        glu_tile(i)
                    conv_pair(0)
                    dve.wait_ge(sem("const_landed"), 32)
                    dve.wait_ge(sem("act_gate"), 3)
                    nc.vector.tensor_scalar(flat["z"], flat["z"], 0.0, None, ALU.min).then_inc(sem("gate"), 1)
                    dve.wait_ge(sem("gate"), 1)
                    nc.vector.tensor_tensor(flat["z"], flat["z"], flat["za"], ALU.subtract).then_inc(sem("gate"), 1)
                    dve.wait_ge(sem("gate"), 2)
                    for f in range(GF):
                        nc.vector.tensor_tensor_scan(gf["bc"][:, f, :], cst[:, CONST["scan"]], gf["z"][:, f, :], 0.0,
                                                     ALU.mult, ALU.add).then_inc(sem("bc_made"), 1)
                    dve.wait_ge(sem("bc_made"), GF)
                    bcc = cut(A_MEM, "bc", "p (c t) -> p c t", t=CHUNK)
                    edc = cut(A_MEM, "ed", "p (c t) -> p c t", t=CHUNK)
                    half = GF * NCHUNK // 2
                    for i in range(2):
                        cs = slice(i * half, (i + 1) * half)
                        nc.vector.tensor_tensor(edc[:, cs, :],
                                                bcc[:, cs, CHUNK - 1:CHUNK].broadcast_to([P, half, CHUNK]),
                                                bcc[:, cs, :], ALU.subtract).then_inc(sem("bd_made"), 1)
                    conv_pair(2)
                    dve.wait_ge(sem("att_zeroed"), 1)
                    for n in range(8):
                        dve.wait_ge(sem("att_filled"), n // 4 + 1)
                        nc.vector.copy_predicated(att[:, n, :], mask[:, :], M[n // 4][:, (n % 4) * P:(n % 4 + 1) * P]
                                                  ).then_inc(sem("att_masked"), 1)
                    ep4 = cut(A_MEM, "ep", "p (f t) -> p f t", f=GF)
                    dve.wait_ge(sem("ep_made"), 1)
                    ins = nc.vector.tensor_copy(st[:, 0, :, :].rearrange("p f n -> p (f n)"),
                                                rd.full("upd", 0)[:, 0:GF * GV])
                    rd.free(ins, "upd", 0)
                    for c in range(1, NCHUNK - 1):
                        bank = rd.full("upd", c)
                        rd.read_wait("upd", c - 1)
                        if c > 1:
                            dve.wait_ge(sem("state_half"), c - 1)
                        nc.vector.scalar_tensor_tensor(
                            out=st[:, c, 0, :], in0=st[:, c - 1, 0, :],
                            scalar=ep4[:, 0, (c + 1) * CHUNK - 1:(c + 1) * CHUNK], in1=bank[:, 0:GV],
                            op0=ALU.mult, op1=ALU.add).then_inc(sem("state_half"), 1)
                        ins = nc.vector.scalar_tensor_tensor(
                            out=st[:, c, 1, :], in0=st[:, c - 1, 1, :],
                            scalar=ep4[:, 1, (c + 1) * CHUNK - 1:(c + 1) * CHUNK], in1=bank[:, GV:2 * GV],
                            op0=ALU.mult, op1=ALU.add)
                        rd.free(ins, "upd", c)
                    norm_dve(dve, "cln", cy, CF)
                    for p in range(2):
                        dve.wait_ge(sem("rms_sd"), p + 1)
                        pair = rs[:, 2 * p:2 * p + 2, :].rearrange("p h t -> p (h t)")
                        nc.vector.reciprocal(pair, pair).then_inc(sem("rms_r"), 1)
                    rd.read_wait("o", GH - 1)
                    dve.wait_ge(sem("rms_r"), 2)
                    for h in range(GH):
                        rd.read_wait("o", h)
                        nc.vector.tensor_tensor(o[:, h, :], o[:, h, :], rs[:, h, :], ALU.mult
                                                ).then_inc(sem("o_scaled"), 1)
                    for h in range(GH):
                        dve.wait_ge(sem("o_scaled"), h + 1)
                        rd.read_wait("r", h)
                        nc.vector.scalar_tensor_tensor(out=mix[:, CF + h, :], in0=o[:, h, :],
                                                       scalar=vcol(va, VEC_A, "gla_g"), in1=r[:, h, :],
                                                       op0=ALU.mult, op1=ALU.mult).then_inc(sem("gated"), 1)

                    dve.wait_ge(sem("c_ready"), 1)

                    def modulation(i):
                        n = A_PANELS.index(("mod", i))
                        dve.wait_ge(sem(f"panel_landed{n % SLOTS}"), panels_landed(n))
                        for j in range(4):
                            w = ring[:, (n % SLOTS) * PANEL + j * D:(n % SLOTS) * PANEL + (j + 1) * D]
                            f = 4 * i + j
                            for c in ((1, 0) if f < 2 * KD else (0,)):
                                if c:
                                    if f:
                                        dve.wait_ge(sem("ctx_summed"), f)
                                    nc.vector.tensor_tensor_reduce(
                                        out=cut(A_MEM, "junk"), in0=w, in1=cond[:, 1, :], scale=1.0, scalar=0.0,
                                        op0=ALU.mult, op1=ALU.add, accum_out=mod_sum[:, f, 1:2]
                                        ).then_inc(sem("ctx_summed"), 1)
                                else:
                                    ins = nc.vector.tensor_tensor_reduce(
                                        out=w, in0=w, in1=cond[:, 0, :], scale=1.0, scalar=0.0,
                                        op0=ALU.mult, op1=ALU.add, accum_out=mod_sum[:, f, 0:1])
                        ins.then_inc(sem("mod_summed"), 1)

                    def residual(stage, ln, extra=None):
                        for f in range(KD):
                            bank = rd.full(stage, f)
                            ins = nc.vector.scalar_tensor_tensor(out=x3[:, f, :], in0=x3[:, f, :], scalar=ALPHA,
                                                                 in1=bank[:, 0:T], op0=ALU.mult, op1=ALU.add)
                            rd.free(ins, stage, f)
                            if extra and f in extra:
                                modulation(extra[f])
                        for f in range(KD):
                            rd.read_wait(stage, f)
                        norm_dve(dve, ln, x3, KD)

                    residual("mix", "ln1")
                    modulation(0)
                    for i in range(8):
                        bank = rd.full("sc", i)
                        nc.vector.tensor_reduce(nmax[:, i:i + 1], bank[:, 0:T], AX_X, ALU.max, negate=True
                                                ).then_inc(sem("nmax_made"), 1)
                    for i in range(8):
                        rd.read_wait("sc", i)
                        nc.vector.reciprocal(rinv[:, i:i + 1], rsum[:, i:i + 1]).then_inc(sem("rinv_made"), 1)
                        dve.wait_ge(sem("rinv_made"), i + 1)
                        nc.vector.tensor_scalar(px[:, i, :], px[:, i, :], rinv[:, i:i + 1], None, ALU.mult
                                                ).then_inc(sem("px_made"), 1)
                    for f in range(KD):
                        ins = nc.vector.tensor_copy(oxx[:, f, :], rd.full("ox", f)[:, 0:T])
                        rd.free(ins, "ox", f)
                    residual("xo", "ln2")
                    for i in range(KF):
                        rd.read_wait("fi", 2 * i)
                        ins = nc.vector.tensor_tensor(hid[:, i, :], rd.full("fi", 2 * i + 1)[:, 0:T], sg[:, i % 4, :],
                                                      ALU.mult)
                        rd.free(ins, "fi", 2 * i + 1)
                        if i % 2 and i // 2 < 8:
                            modulation(1 + i // 2)
                    residual("fo", "ln3", {0: 9, 2: 10, 4: 11})
                    dve.wait_ge(sem("mod_summed"), 12)
                    dst = modT[:, bass.ds(layer * 96, 96)].rearrange("p (j c) -> p j c", c=2)
                    nc.vector.tensor_tensor(dst, mod_sum,
                                            va[:, VEC_A["b_mod"]].unsqueeze(2).broadcast_to([P, 48, 2]), ALU.add)
            clear_semaphores()

        lng, lnb = VEC_B["ln_g"].start, VEC_B["ln_b"].start
        POST = {"g": slice(lng, lng + 32), "b": slice(lnb, lnb + 32)}
        ht = memT[:, :].rearrange("p (a n) -> p a n", a=TT)
        hp = cut(Q_MEM, "hp", "p (f t) -> p f t", f=KD)
        pq = cut(Q_MEM, "pq", "p (j t) -> p j t", j=16)
        s12 = cut(P_MEM, "s12", "p (a n) -> p a n", a=TT)

        def mod_part(l, part, f, c=0):
            return mod4[:, l, part * KD + f, c:c + 1]

        slot = cut(P_MEM, "ring", "p (s n) -> p s n", s=RING)
        scores = cut(P_MEM, "s12", "p (n b k) -> p n b k", n=TT * PH, b=2)
        wk = cut(P_MEM, "wk", "p (b n) -> p b n", b=2)
        v16 = cut(P_MEM, "v16", "p (b k) -> p b k", b=2)
        i16 = cut(P_MEM, "i16").bitcast(U32).rearrange("p (b k) -> p b k", b=2)
        i16f = cut(P_MEM, "if", "p (b k) -> p b k", b=2)
        cand = cut(P_MEM, "cand", "p (i j) -> p i j", i=TOPK)
        cw = cut(P_MEM, "cw")
        top = cut(P_MEM, "top")
        pos = cut(P_MEM, "pos").bitcast(U32)
        ab = cut(P_MEM, "ab").bitcast(U32).rearrange("p (b k) -> p b k", b=2)
        abf = cut(P_MEM, "abf", "p (b k) -> p b k", b=2)
        oh = cut(P_MEM, "oh", "p (k i) -> p k i", k=TOPK)
        selected = cut(P_MEM, "sel", "p (b k) -> p b k", b=2)
        idf = cut(P_MEM, "idf")
        idx = cut(P_MEM, "idx").bitcast(U32).rearrange("p (h k) -> p h k", h=2)
        gate = cut(P_MEM, "gate", "p (h k) -> p h k", h=2)
        gs = cut(P_MEM, "gs")
        dot, gelu = cut(P_MEM, "dot"), cut(P_MEM, "act")
        diag = cut(P_MEM, "diag", "p (s n) -> p s n", s=NDIAG)
        iota = cst[:, CONST["iota"]]

        class Chain:

            def __init__(self, dve):
                self.dve, self.done = dve, 0

            def __call__(self, ins):
                self.done += 1
                ins.then_inc(sem("step"), 1)
                self.dve.wait_ge(sem("step"), self.done)

            def best16(self, values, index, src, work):
                self(nc.vector.max(values[:, 0:8], src))
                self(nc.vector.max_index(index[:, 0:8], values[:, 0:8], src))
                self(nc.vector.match_replace(work, values[:, 0:8], src, NEG))
                self(nc.vector.max(values[:, 8:16], work))
                self(nc.vector.max_index(index[:, 8:16], values[:, 8:16], work))

        def select(chain, part, n, l):
            if part in (0, 1):
                chain.best16(v16[:, part, :], i16[:, part, :], scores[:, n, part, :], wk[:, part, :])
            if part == 2:
                chain(nc.vector.tensor_copy(i16f, i16))
                chain(nc.vector.tensor_tensor(cand, v16[:, 0, :].unsqueeze(2).broadcast_to([P, TOPK, TOPK]),
                                              v16[:, 1, :].unsqueeze(1).broadcast_to([P, TOPK, TOPK]), ALU.add))
            if part == 3:
                chain.best16(top, pos, cand.rearrange("p i j -> p (i j)"), cw)
                nc.vector.tensor_scalar(gs[:, 0:1], top[:, 0:1], -1.0, None, ALU.mult).then_inc(sem("top_made"), 1)
            if part == 4:
                chain(nc.vector.tensor_scalar(ab[:, 0, :], pos, 4, None, ALU.logical_shift_right))
                chain(nc.vector.tensor_scalar(ab[:, 1, :], pos, 15, None, ALU.bitwise_and))
                chain(nc.vector.tensor_copy(abf, ab))
            if part in (4, 5):
                b = part - 4
                chain(nc.vector.tensor_tensor(oh, abf[:, b, :].unsqueeze(2).broadcast_to([P, TOPK, TOPK]),
                                              iota.unsqueeze(1).broadcast_to([P, TOPK, TOPK]), ALU.is_equal))
                chain(nc.vector.tensor_tensor(oh, oh, i16f[:, b, :].unsqueeze(1).broadcast_to([P, TOPK, TOPK]),
                                              ALU.mult))
                chain(nc.vector.tensor_reduce(selected[:, b, :], oh, AX_X, ALU.add))
            if part == 5:
                chain(nc.vector.scalar_tensor_tensor(out=idf, in0=selected[:, 0, :], scalar=float(NK),
                                                     in1=selected[:, 1, :], op0=ALU.mult, op1=ALU.add))
                nc.vector.tensor_scalar(idx[:, n % 2, :], idf, float(l * NEXP), None, ALU.add
                                        ).then_inc(sem("idx_made"), 1)
            if part == 6:
                chain.dve.wait_ge(sem("gate_exp"), max(n, 1))
                chain(nc.vector.reciprocal(gs[:, 2:3], gs[:, 1:2]))
                chain(nc.vector.tensor_scalar(gate[:, n % 2, :], gate[:, n % 2, :], gs[:, 2:3], None, ALU.mult))

        def gate_exp(act, n):
            act.wait_ge(sem("top_made"), max(n, 1))
            nc.scalar.activation(gate[:, n % 2, :], top, ACT.Exp, bias=gs[:, 0:1], accum_out=gs[:, 1:2]
                                 ).then_inc(sem("gate_exp"), 1)

        def gather(pool, s):
            n, k = s // TOPK, s % TOPK
            pool.indirect_dma_start(slot[:, s % RING, :], None, tables,
                                    bass.IndirectOffsetOnAxis(idx[:, n % 2, k:k + 1], 0)
                                    ).then_inc(sem(f"row_landed{s % RING}"), 16)

        def peer_prep_pe(e, rd):
            def queries(i):
                e.feature_tiles(e.panel("pq", i), "pq", 4 * i, 4, KD, hp, T,
                                None if i else lambda k: e.pe.wait_ge(sem("hp_made"), k + 1))

            def key_scores(i):
                a, g = i // 4, i % 4
                for j in range(4):
                    rd.read_wait("pq", 4 * g + j)
                bank = e.bank("ps", i)
                for j in range(4):
                    n = 4 * g + j
                    ins = nc.tensor.matmul(bank[:, j * P:(j + 1) * P], pq[:, n, a * P:(a + 1) * P],
                                           keys[:, n * P:(n + 1) * P], start=True, stop=True)
                e.filled(ins, "ps", i)

            queries(0)
            keys = e.panel("pk", 0)
            key_scores(0)
            for i in range(1, 4):
                queries(i)
            for i in range(4):
                bank = e.bank("ht", i)
                for j in range(4):
                    f = (i % 2) * 4 + j
                    ins = nc.tensor.transpose(bank[:, j * P:(j + 1) * P], hp[:, f, (i // 2) * P:(i // 2 + 1) * P],
                                              ident)
                e.filled(ins, "ht", i)
            for i in range(1, 8):
                key_scores(i)

        def peer_prep_act(act, rd):
            for i in range(16):
                ins = nc.scalar.activation(pq[:, i, :], rd.full("pq", i)[:, 0:T], ACT.Copy)
                rd.free(ins, "pq", i)
            gate_exp(act, 0)

        def modulated_dve(dst, l, part, signal, f):
            nc.vector.tensor_scalar(dst, x3[:, f, :], mod_part(l, part + 1, f), mod_part(l, part, f),
                                    ALU.mult, ALU.add).then_inc(sem(signal), 1)

        def peer_prep_dve(dve, rd, l, ln):
            for f in range(KD):
                dve.wait_ge(sem(f"{ln}_out"), f + 1)
                modulated_dve(hp[:, f, :], l, 3, "hp_made", f)

            def key_scores(i):
                ins = nc.vector.tensor_copy(s12[:, i // 4, (i % 4) * 512:(i % 4 + 1) * 512], rd.full("ps", i)[:, :])
                rd.free(ins, "ps", i)

            chain = Chain(dve)
            key_scores(0)
            rd.read_wait("ps", 0)
            for part in range(6):
                select(chain, part, 0, l)
            for i in range(4):
                ins = nc.vector.tensor_copy(ht[:, i // 2, (i % 2) * 512:(i % 2 + 1) * 512], rd.full("ht", i)[:, :])
                rd.free(ins, "ht", i)
            for i in range(1, 8):
                key_scores(i)
            select(chain, 6, 0, l)

        def peer_prep_pool(pool):
            pool.wait_ge(sem("idx_made"), 1)
            for s in range(RING):
                gather(pool, s)

        def gated_act(act, rd, stage, l, part):
            gated = sq
            for f in range(KD):
                ins = nc.scalar.activation(gated[:, f, :], rd.full(stage, f)[:, 0:T], ACT.Copy,
                                           scale=mod_part(l, part, f))
                rd.free(ins, stage, f)

        def gated_residual_dve(dve, wait, signal):
            for f in range(KD):
                wait(f)
                nc.vector.scalar_tensor_tensor(out=x3[:, f, :], in0=x3[:, f, :], scalar=ALPHA, in1=sq[:, f, :],
                                               op0=ALU.mult, op1=ALU.add).then_inc(sem(signal), 1)
            dve.wait_ge(sem(signal), KD)

        hh = cut(B_MEM, "h", "p (f t) -> p f t", f=KD)
        cq = cut(B_MEM, "cq", "p (f t) -> p f t", f=3)
        ckv = cut(B_MEM, "ckv", "p (f t) -> p f t", f=2)
        kr = cut(B_MEM, "kr", "p (f t) -> p f t", f=2)
        kro = cut(B_MEM, "kro", "p (f t) -> p f t", f=2)
        qr = cut(B_MEM, "qr", "p (f t) -> p f t", f=4)
        qro = cut(B_MEM, "qro", "p (f t) -> p f t", f=4)
        qn = cut(B_MEM, "qn", "p (f t) -> p f t", f=MH)
        kn = cut(B_MEM, "kn", "p (f t) -> p f t", f=MH)
        vm = cut(B_MEM, "vm", "p (m n) -> p m n", m=4)
        tm = cut(B_MEM, "tmp", "p (f t) -> p f t", f=2)
        pb = cut(B_MEM, "p", "p (a t) -> p a t", a=2)
        ptb = cut(B_MEM, "pt", "p (a m t) -> p m a t", a=2, m=4)
        ptb_flat = cut(B_MEM, "pt", "p (a n) -> p a n", a=2)
        oxb = arena[:, B_OX:B_OX + KD * T].rearrange("p (f t) -> p f t", f=KD)
        cos, sin = cst[:, CONST["cos"]], cst[:, CONST["sin"]]
        MSCALE = (NOPE + ROPE) ** -0.5
        ROT = MH * ROPE // 2 // P

        with nc.Block() as block:
            @block.sync
            def _(sp):
                sp.dma_start(hh[:, :, T:2 * T], acts[2].rearrange("p (f t) -> p f t", f=KD)
                             ).then_inc(sem("ctx_landed"), 16)
                stream(sp, B_PANELS, B_TILES, DEPTH * len(A_PANELS), False)

            @block.tensor
            def _(pe):
                e = PE(pe, B_PANELS, B_TILES)
                rd = Reader(pe, B_TILES)
                w = e.panel("zi", 0)
                e.feature_tiles(w, "zi", 0, 3, KD, hh, T, lambda k: pe.wait_ge(sem("h_made"), k + 1))
                e.feature_tiles(w[:, 3 * KD * P:], "zi", 3, 1, KD, hh, 2 * T,
                                lambda k: pe.wait_ge(sem("hc_made"), k + 1))
                e.feature_tiles(e.panel("zi", 1), "zi", 4, 3, KD, hh, 2 * T)
                for f in range(3):
                    pe.wait_ge(sem("lsq_made"), f + 1)
                    ins = nc.tensor.matmul(M[0][:, 0:T], ones[:, :], sq[:, f, :], start=(f == 0), stop=(f == 2))
                ins.then_inc(sem("rms_filled"), 1)
                for f in range(2):
                    pe.wait_ge(sem("lsq_made"), f + 4)
                    ins = nc.tensor.matmul(M[1][:, :], ones[:, :],
                                           sq[:, 3 + 2 * f:5 + 2 * f, :].rearrange("p a t -> p (a t)"),
                                           start=(f == 0), stop=(f == 1))
                ins.then_inc(sem("rms_filled"), 1)
                pe.wait_ge(sem("cq_normed"), 3)
                for i in range(2):
                    e.feature_tiles(e.panel("uq", i), "uq", 6 * i, 6, 3, cq, T)
                pe.wait_ge(sem("ckv_normed"), 2)
                w = e.panel("ukv", 0)
                e.feature_tiles(w, "kn", 0, MH, 2, ckv, 2 * T)
                for c in range(2):
                    e.token_tiles(w, "vm", 4 * c, 4, 2, ckv, width=D, off=MH * 2 * P + c * 512)
                pe.wait_ge(sem("q_rotated"), 2 * ROT)
                pe.wait_ge(sem("k_rotated"), 2)

                def scores(h):
                    rd.read_wait("uq", h)
                    rd.read_wait("kn", h)
                    rows = slice((h % 4) * 32, (h % 4 + 1) * 32)
                    for a in range(TT):
                        bank = e.bank("sc", 2 * h + a)
                        cols = slice(a * P, (a + 1) * P)
                        nc.tensor.matmul(bank[:, :], qn[:, h, cols], kn[:, h, :], start=True, stop=False)
                        for k in range(2):
                            ins = nc.tensor.matmul(bank[:, :], qro[rows, k * ROT + h // 4, cols], kro[rows, k, :],
                                                   start=False, stop=(k == 1),
                                                   tile_position=((h % 4) * 32, 0))
                        e.filled(ins, "sc", 2 * h + a)

                def values(h):
                    for a in range(TT):
                        pe.wait_ge(sem("p_made"), 2 * h + a + 1)
                        bank = e.bank("pt", 2 * h + a)
                        for m in range(4):
                            ins = nc.tensor.transpose(bank[:, m * P:(m + 1) * P], pb[:, a, m * P:(m + 1) * P], ident)
                        e.filled(ins, "pt", 2 * h + a)
                    for a in range(TT):
                        rd.read_wait("pt", 2 * h + a)
                    bank = e.bank("ox", h)
                    for a in range(TT):
                        for m in range(4):
                            ins = nc.tensor.matmul(bank[:, a * P:(a + 1) * P], vm[:, m, h * VD:(h + 1) * VD],
                                                   ptb[:, m, a, :], start=(m == 0), stop=(m == 3))
                    e.filled(ins, "ox", h)

                for i in range(8):
                    rd.read_wait("vm", i)
                for h in range(MH):
                    scores(h)
                    if h:
                        values(h - 1)
                values(MH - 1)
                for i in range(2):
                    e.feature_tiles(e.panel("wo", i), "wo", 4 * i, 4, KD, oxb, T,
                                    None if i else lambda k: rd.read_wait("ox", k))
                norm_pe(pe, "lnb", lambda f: pe.wait_ge(sem("res_made"), f + 1), x3, KD)
                peer_prep_pe(e, rd)

            @block.scalar
            def _(act):
                rd = Reader(act, B_TILES)
                act.wait_ge(sem("mod_ready"), 1)
                act.wait_ge(sem("ctx_landed"), 16)
                for f in range(KD):
                    nc.scalar.activation(hh[:, f, T:2 * T], hh[:, f, T:2 * T], ACT.Identity,
                                         scale=mod_part(0, 1, f, 1), bias=mod_part(0, 0, f, 1)
                                         ).then_inc(sem("hc_made"), 1)
                for i in range(3):
                    bank = rd.full("zi", i)
                    nc.scalar.activation(sq[:, i, :], bank[:, 0:T], ACT.Square).then_inc(sem("lsq_made"), 1)
                    rd.free(nc.scalar.activation(cq[:, i, :], bank[:, 0:T], ACT.Copy), "zi", i)
                for i in range(2):
                    bank = rd.full("zi", 3 + i)
                    nc.scalar.activation(sq[:, 3 + 2 * i:5 + 2 * i, :].rearrange("p a t -> p (a t)"), bank[:, :],
                                         ACT.Square).then_inc(sem("lsq_made"), 1)
                    rd.free(nc.scalar.activation(ckv[:, i, :], bank[:, :], ACT.Copy), "zi", 3 + i)
                for i in range(2):
                    rd.free(nc.scalar.activation(kr[:, i, :], rd.full("zi", 5 + i)[:, :], ACT.Copy), "zi", 5 + i)
                act.wait_ge(sem("rms_filled"), 1)
                nc.scalar.activation(sd, M[0][:, 0:T], ACT.Sqrt, scale=1.0 / QL, bias=eps[:, 1:2]
                                     ).then_inc(sem("rms_sd"), 1)
                act.wait_ge(sem("rms_filled"), 2)
                nc.scalar.activation(tm[:, 0, :], M[1][:, :], ACT.Sqrt, scale=1.0 / KVL, bias=eps[:, 1:2]
                                     ).then_inc(sem("rms_sd"), 1)
                for i in range(12):
                    dst = qn[:, i, :] if i < MH else qr[:, i - MH, :]
                    rd.free(nc.scalar.activation(dst, rd.full("uq", i)[:, 0:T], ACT.Copy), "uq", i)
                for i in range(MH):
                    rd.free(nc.scalar.activation(kn[:, i, :], rd.full("kn", i)[:, :], ACT.Copy), "kn", i)

                def softmax(h):
                    for a in range(TT):
                        n = 2 * h + a
                        bank = rd.full("sc", n)
                        act.wait_ge(sem("nmax_scaled"), n + 1)
                        if h:
                            rd.full("pt", n - 2)
                        ins = nc.scalar.activation(pb[:, a, :], bank[:, :], ACT.Exp, scale=MSCALE,
                                                   bias=nmax[:, n:n + 1], accum_out=rsum[:, n:n + 1])
                        rd.free(ins, "sc", n)

                for h in range(MH):
                    softmax(h)
                    for a in range(TT):
                        n = 2 * h + a
                        if h:
                            rd.full("ox", h - 1)
                        rd.free(nc.scalar.activation(ptb_flat[:, a, :], rd.full("pt", n)[:, :], ACT.Copy), "pt", n)
                gated_act(act, rd, "wo", 0, 2)
                norm_act(act, "lnb", KD, x3, vb, POST, "g", "b", off=0)
                peer_prep_act(act, rd)

            @block.vector
            def _(dve):
                rd = Reader(dve, B_TILES)
                scales = modT[:, :].rearrange("p (l q j) -> p l q j", l=DEPTH, q=6)
                for part in (1, 4):
                    ins = nc.vector.tensor_scalar(scales[:, :, part, :], scales[:, :, part, :], 1.0, None, ALU.add)
                    ins.then_inc(sem("mod_half" if part == 1 else "mod_ready"), 1)
                dve.wait_ge(sem("mod_ready"), 1)
                dve.wait_ge(sem("mod_half"), 1)
                for f in range(KD):
                    modulated_dve(hh[:, f, 0:T], 0, 0, "h_made", f)

                def rotate(out1, out2, x1, x2, c, s, signal):
                    n = x1.shape[-1]
                    t1, t2 = xc[:, 0:2, :].rearrange("p a t -> p (a t)")[:, 0:n], \
                        xc[:, 2:4, :].rearrange("p a t -> p (a t)")[:, 0:n]
                    nonlocal turned
                    for o_, a_, b_, op in ((out1, c, s, ALU.subtract), (out2, s, c, ALU.add)):
                        nc.vector.tensor_tensor(t1, x1, a_, ALU.mult).then_inc(sem("turned"), 1)
                        nc.vector.tensor_tensor(t2, x2, b_, ALU.mult).then_inc(sem("turned"), 1)
                        turned += 2
                        dve.wait_ge(sem("turned"), turned)
                        signalled[signal] = signalled.get(signal, 0) + 1
                        nc.vector.tensor_tensor(o_, t1, t2, op).then_inc(sem(signal), 1)
                        dve.wait_ge(sem(signal), signalled[signal])

                turned, signalled = 0, {}
                for i in range(2):
                    rd.read_wait("zi", 5 + i)
                rotate(kro[:, 0, :], kro[:, 1, :], kr[:, 0, :], kr[:, 1, :], cos, sin, "k_rotated")
                dve.wait_ge(sem("rms_sd"), 1)
                nc.vector.reciprocal(rstd, sd).then_inc(sem("rms_r"), 1)
                dve.wait_ge(sem("rms_r"), 1)
                for i in range(3):
                    rd.read_wait("zi", i)
                    nc.vector.scalar_tensor_tensor(out=cq[:, i, :], in0=cq[:, i, :], scalar=vcol(vb, VEC_B, "q_norm", i),
                                                   in1=rstd, op0=ALU.mult, op1=ALU.mult
                                                   ).then_inc(sem("cq_normed"), 1)
                dve.wait_ge(sem("rms_sd"), 2)
                nc.vector.reciprocal(tm[:, 1, :], tm[:, 0, :]).then_inc(sem("rms_r"), 1)
                dve.wait_ge(sem("rms_r"), 2)
                for i in range(2):
                    rd.read_wait("zi", 3 + i)
                    nc.vector.scalar_tensor_tensor(out=ckv[:, i, :], in0=ckv[:, i, :],
                                                   scalar=vcol(vb, VEC_B, "kv_norm", i), in1=tm[:, 1, :],
                                                   op0=ALU.mult, op1=ALU.mult).then_inc(sem("ckv_normed"), 1)
                for i in range(ROT):
                    rd.read_wait("uq", MH + i)
                    rd.read_wait("uq", MH + ROT + i)
                    rotate(qro[:, i, :], qro[:, ROT + i, :], qr[:, i, :], qr[:, ROT + i, :], cos[:, 0:T], sin[:, 0:T],
                           "q_rotated")
                for i in range(8):
                    rd.free(nc.vector.tensor_copy(vm[:, i % 4, (i // 4) * 512:(i // 4 + 1) * 512],
                                                  rd.full("vm", i)[:, :]), "vm", i)

                def peak(h):
                    for a in range(TT):
                        n = 2 * h + a
                        nc.vector.tensor_reduce(nmax[:, n:n + 1], rd.full("sc", n)[:, :], AX_X, ALU.max, negate=True
                                                ).then_inc(sem("nmax_made"), 1)
                        dve.wait_ge(sem("nmax_made"), n + 1)
                        nc.vector.tensor_scalar(nmax[:, n:n + 1], nmax[:, n:n + 1], MSCALE, None, ALU.mult
                                                ).then_inc(sem("nmax_scaled"), 1)

                for h in range(MH):
                    peak(h)
                    for a in range(TT):
                        n = 2 * h + a
                        rd.read_wait("sc", n)
                        nc.vector.reciprocal(rinv[:, n:n + 1], rsum[:, n:n + 1]).then_inc(sem("rinv_made"), 1)
                        dve.wait_ge(sem("rinv_made"), n + 1)
                        nc.vector.tensor_scalar(pb[:, a, :], pb[:, a, :], rinv[:, n:n + 1], None, ALU.mult
                                                ).then_inc(sem("p_made"), 1)
                    if h:
                        rd.free(nc.vector.tensor_copy(oxb[:, h - 1, :], rd.full("ox", h - 1)[:, 0:T]), "ox", h - 1)
                rd.free(nc.vector.tensor_copy(oxb[:, MH - 1, :], rd.full("ox", MH - 1)[:, 0:T]), "ox", MH - 1)
                gated_residual_dve(dve, lambda f: rd.read_wait("wo", f), "res_made")
                norm_dve(dve, "lnb", x3, KD)
                peer_prep_dve(dve, rd, 0, "lnb")

            @block.gpsimd
            def _(pool):
                peer_prep_pool(pool)
        clear_semaphores()

        def peer(l):
            heads = TT * PH
            base = l * heads * (16 * TOPK // RING)

            with nc.Block() as block:
                @block.gpsimd
                def _(pool):
                    for s in range(RING, heads * TOPK):
                        if s % TOPK == 0:
                            pool.wait_ge(sem("idx_made"), s // TOPK)
                        pool.wait_ge(sem("row_used"), s - RING + 1)
                        gather(pool, s)

                @block.scalar
                def _(act):
                    for s in range(0, heads * TOPK, PAIR):
                        n, c = s // TOPK, s % (2 * TOPK)
                        act.wait_ge(sem("dot_made"), s + PAIR)
                        nc.scalar.activation(gelu[:, c:c + PAIR], dot[:, c:c + PAIR], ACT.Gelu
                                             ).then_inc(sem("gelu_made"), 1)
                        if s % TOPK // PAIR == 4 and n + 1 < heads:
                            gate_exp(act, n + 1)

                @block.tensor
                def _(pe):
                    for s in range(heads * TOPK):
                        a, first, last = s // (PH * TOPK), s % (PH * TOPK) == 0, (s + 1) % (PH * TOPK) == 0
                        pe.wait_ge(sem("diag_made"), s + 1)
                        for b in range(2):
                            ins = nc.tensor.matmul(M[2 * a + b][:, :], diag[:, s % NDIAG, :],
                                                   slot[:, s % RING, D + b * 512:D + (b + 1) * 512],
                                                   start=first, stop=last)
                        ins.then_inc(sem("row_used"), 1)

                @block.vector
                def _(dve):
                    chain = Chain(dve)

                    def diagonals(s0):
                        dve.wait_ge(sem("gelu_made"), s0 // PAIR + 1)
                        for s in range(s0, s0 + PAIR):
                            n, k, c = s // TOPK, s % TOPK, s % (2 * TOPK)
                            if s >= NDIAG:
                                dve.wait_ge(sem("row_used"), s - NDIAG + 1)
                            nc.vector.tensor_scalar(diag[:, s % NDIAG, :], ident, gelu[:, c:c + 1],
                                                    gate[:, n % 2, k:k + 1], ALU.mult, ALU.mult
                                                    ).then_inc(sem("diag_made"), 1)

                    def close_tile(a):
                        dve.wait_ge(sem("row_used"), (a + 1) * PH * TOPK)
                        for b in range(2):
                            nc.vector.tensor_copy(ht[:, a, b * 512:(b + 1) * 512], M[2 * a + b][:, :])

                    for s0 in range(0, heads * TOPK, PAIR):
                        n = s0 // TOPK
                        for s in range(s0, s0 + PAIR):
                            c = s % (2 * TOPK)
                            dve.wait_ge(sem(f"row_landed{s % RING}"), base + 16 * (s // RING + 1))
                            u = slot[:, s % RING, 0:D]
                            nc.vector.tensor_tensor_reduce(out=u, in0=u, in1=ht[:, n // PH, :], scale=1.0, scalar=0.0,
                                                           op0=ALU.mult, op1=ALU.add, accum_out=dot[:, c:c + 1]
                                                           ).then_inc(sem("dot_made"), 1)
                        if n + 1 < heads and s0 % TOPK // PAIR < 7:
                            select(chain, s0 % TOPK // PAIR, n + 1, l)
                        if s0:
                            diagonals(s0 - PAIR)
                        if s0 % (PH * TOPK) == 0 and s0:
                            close_tile(s0 // (PH * TOPK) - 1)
                    diagonals(heads * TOPK - PAIR)
                    close_tile(TT - 1)
            clear_semaphores()

        def peer_out_pe(pe):
            for i in range(4):
                for j in range(2):
                    f = 2 * i + j
                    for a in range(TT):
                        ins = nc.tensor.transpose(T_[i][:, j * T + a * P:j * T + (a + 1) * P],
                                                  ht[:, a, f * P:(f + 1) * P], ident)
                ins.then_inc(sem("sum_turned"), 1)

        def peer_out_block(l):
            with nc.Block() as block:
                @block.tensor
                def _(pe):
                    peer_out_pe(pe)
                    norm_pe(pe, "lnp", lambda f: pe.wait_ge(sem("res_made"), f + 1), x3, KD)

                @block.scalar
                def _(act):
                    for f in range(KD):
                        act.wait_ge(sem("sum_turned"), f // 2 + 1)
                        nc.scalar.activation(sq[:, f, :], T_[f // 2][:, (f % 2) * T:(f % 2 + 1) * T], ACT.Copy,
                                             scale=mod_part(l, 5, f)).then_inc(sem("gated"), 1)
                    norm_act(act, "lnp", KD, x3, vb, POST, "g", "b", off=(2 * l + 1) * KD)

                @block.vector
                def _(dve):
                    gated_residual_dve(dve, lambda f: dve.wait_ge(sem("gated"), f + 1), "res_made")
                    norm_dve(dve, "lnp", x3, KD)

                @block.sync
                def _(sp):
                    if l < DEPTH - 1:
                        first_panels(sp, DEPTH * len(A_PANELS) + len(B_PANELS))
                    else:
                        sp.wait_ge(sem("lnp_out"), KD)
                        sp.dma_start(out, xT[:, :]).then_inc(sem("out_written"), 16)
                        sp.wait_ge(sem("out_written"), 16)
            if l < DEPTH - 1:
                clear_semaphores()

        peer(0)
        peer_out_block(0)

        PAD = max(WINDOWS) // 2
        W = T + 2 * PAD
        hc3 = cut(C_MEM, "pooled", "p (f t) -> p f t", f=KD)
        zp = cut(C_MEM, "zp", "p (f t) -> p f t", f=KD)
        s1 = cut(C_MEM, "s1", "p (f t) -> p f t", f=2)
        s2 = cut(C_MEM, "s2", "p (f t) -> p f t", f=2)
        yg = cut(C_MEM, "yg", "p (f t) -> p f t", f=KD)
        invcnt = cst[:, CONST["invcnt"]].rearrange("p (g t) -> p g t", g=GROUPS)

        with nc.Block() as block:
            @block.sync
            def _(sp):
                stream(sp, C_PANELS, C_TILES, DEPTH * len(A_PANELS) + len(B_PANELS), False)

            @block.gpsimd
            def _(pool):
                nc.gpsimd.memset(zp[:, :, 0:PAD], 0.0).then_inc(sem("pad_set"), 1)
                nc.gpsimd.memset(zp[:, :, PAD + T:], 0.0).then_inc(sem("pad_set"), 1)
                peer_prep_pool(pool)

            @block.tensor
            def _(pe):
                e = PE(pe, C_PANELS, C_TILES)
                rd = Reader(pe, C_TILES)

                def modulated(k):
                    pe.wait_ge(sem("odd_made" if k % 2 else "even_made"), k // 2 + 1)

                for i in range(2):
                    e.feature_tiles(e.panel("pin", i), "pin", 4 * i, 4, KD, hc3, T, None if i else modulated)
                w = e.panel("grp", 0)
                for j in range(KD):
                    g = j // 2
                    pe.wait_ge(sem("pooled"), g + 1)
                    bank = e.bank("grp", j)
                    for k in range(2):
                        ins = nc.tensor.matmul(bank[:, 0:T], w[:, (2 * j + k) * P:(2 * j + k + 1) * P],
                                               hc3[:, 2 * g + k, :], start=(k == 0), stop=(k == 1))
                    e.filled(ins, "grp", j)
                for i in range(2):
                    e.feature_tiles(e.panel("pout", i), "pout", 4 * i, 4, KD, yg, T,
                                    None if i else lambda k: rd.read_wait("grp", k))
                norm_pe(pe, "lnc", lambda f: pe.wait_ge(sem("res_made"), f + 1), x3, KD)
                peer_prep_pe(e, rd)

            @block.scalar
            def _(act):
                rd = Reader(act, C_TILES)
                for f in range(0, KD, 2):
                    nc.scalar.activation(hc3[:, f, :], x3[:, f, :], ACT.Identity, scale=mod_part(1, 1, f),
                                         bias=mod_part(1, 0, f)).then_inc(sem("even_made"), 1)
                for f in range(KD):
                    rd.free(nc.scalar.activation(zp[:, f, PAD:PAD + T], rd.full("pin", f)[:, 0:T], ACT.Copy), "pin", f)
                for f in range(KD):
                    rd.free(nc.scalar.activation(yg[:, f, :], rd.full("grp", f)[:, 0:T], ACT.Copy,
                                                 scale=vcol(vb, VEC_B, "pool_scale", f)), "grp", f)
                gated_act(act, rd, "pout", 1, 2)
                norm_act(act, "lnc", KD, x3, vb, POST, "g", "b", off=2 * KD)
                peer_prep_act(act, rd)

            @block.vector
            def _(dve):
                rd = Reader(dve, C_TILES)
                for f in range(1, KD, 2):
                    modulated_dve(hc3[:, f, :], 1, 0, "odd_made", f)
                dve.wait_ge(sem("pad_set"), 2)
                for f in range(KD):
                    rd.full("pin", f)
                steps = 0
                for g, w in enumerate(WINDOWS):
                    for f in (2 * g, 2 * g + 1):
                        rd.read_wait("pin", f)
                    src, n, size = zp[:, 2 * g:2 * g + 2, :], W, 1
                    dst, other = s1, s2
                    while size < w:
                        n -= size
                        nc.vector.tensor_tensor(dst[:, :, 0:n], src[:, :, 0:n], src[:, :, size:size + n], ALU.add
                                                ).then_inc(sem("doubled"), 1)
                        steps += 1
                        dve.wait_ge(sem("doubled"), steps)
                        src, dst, other, size = dst, other, dst, 2 * size
                    at = PAD - w // 2
                    nc.vector.tensor_tensor(dst[:, :, 0:T], src[:, :, at:at + T],
                                            invcnt[:, g:g + 1, :].broadcast_to([P, 2, T]), ALU.mult
                                            ).then_inc(sem("doubled"), 1)
                    steps += 1
                    dve.wait_ge(sem("doubled"), steps)
                    nc.vector.tensor_tensor(hc3[:, 2 * g:2 * g + 2, :], dst[:, :, 0:T],
                                            zp[:, 2 * g:2 * g + 2, PAD:PAD + T], ALU.subtract
                                            ).then_inc(sem("pooled"), 1)
                    dve.wait_ge(sem("pooled"), g + 1)
                gated_residual_dve(dve, lambda f: rd.read_wait("pout", f), "res_made")
                norm_dve(dve, "lnc", x3, KD)
                peer_prep_dve(dve, rd, 1, "lnc")
        clear_semaphores()
        peer(1)
        peer_out_block(1)


def feature_major(x):
    t, d = x.shape
    return np.ascontiguousarray(x.T.reshape(d // P, P, t).transpose(1, 0, 2)).reshape(P, -1)


def by_partition(v):
    return np.moveaxis(v.reshape(*v.shape[:-1], -1, P), -1, 0).reshape(P, -1)


def feature_panel(w, tiles):
    k = w.shape[0] // P
    parts = [w[:, c].reshape(k, P, P).transpose(1, 0, 2).reshape(P, -1) for c in tiles]
    return pad(np.concatenate(parts, axis=1))


def token_panel(w):
    return pad(w.reshape(-1, P, w.shape[1]).transpose(1, 0, 2).reshape(P, -1))


def pad(w):
    return np.pad(w, ((0, 0), (0, PANEL - w.shape[1])))


def tile(i):
    return slice(i * P, (i + 1) * P)


def lay_out(a):
    panels = []
    cuts = np.cumsum([0, CONV, CONV, GH * GK, GH * GK, GH * GV, GH * GV, RANK])
    for l in range(DEPTH):
        w = a["w_in"][l]
        c_a, c_g, q, k, v, r, _ = (w[:, cuts[i]:cuts[i + 1]] for i in range(7))
        wi, wk, wm = a["w_ffn_in"][l], a["w_xkv"][l], a["w_mod_2"][l]
        made = {
            "glu": lambda i: feature_panel(np.concatenate([x[:, tile(j)] for j in (2 * i, 2 * i + 1) for x in (c_g, c_a)],
                                                          axis=1), [tile(j) for j in range(4)]),
            "qk": lambda i: feature_panel(np.concatenate([q, k], axis=1), [tile(j) for j in range(4)]),
            "v": lambda i: token_panel(v),
            "r": lambda i: feature_panel(r, [tile(j) for j in range(4)]),
            "xk": lambda i: feature_panel(wk, [tile(4 * i + j) for j in range(4)]),
            "xv": lambda i: token_panel(wk[:, D + 512 * i:D + 512 * (i + 1)]),
            "mod": lambda i: wm[:, 512 * i:512 * (i + 1)].T.reshape(4, P, D).transpose(1, 0, 2).reshape(P, -1),
            "fi": lambda i: feature_panel(wi, [tile(c) for j in (2 * i, 2 * i + 1) for c in (j, KF + j)]),
            "fo": lambda i: feature_panel(a["w_ffn_out"][l], [tile(i)]),
            **{s: (lambda w: lambda i: feature_panel(w, [tile(4 * i + j) for j in range(4)]))(a[n][l])
               for s, n in (("mix", "w_mix_out"), ("xq", "w_xq"), ("xo", "w_xo"))},
        }
        panels += [made[s](i) for s, i in A_PANELS]
    wz, wu, wkv = a["mla_w_in_2"][0], a["mla_w_uq_2"][0], a["mla_w_ukv_2"][0]
    kr = wz[:, QL + KVL:]
    half = ROPE // 2
    wz = np.concatenate([wz[:, :QL + KVL]] + [kr[:, :half]] * 4 + [kr[:, half:]] * 4, axis=1)
    wu = wu.reshape(QL, MH, NOPE + ROPE)
    wu = np.concatenate([x.reshape(QL, -1) for x in (wu[:, :, :NOPE], wu[:, :, NOPE:NOPE + half],
                                                     wu[:, :, NOPE + half:])], axis=1)
    wkv = wkv.reshape(KVL, MH, NOPE + VD)
    four = lambda w: lambda i: feature_panel(w, [tile(4 * i + j) for j in range(4)])

    def peer(l):
        k12 = np.stack([a["peer_k1_2"][l], a["peer_k2_2"][l]], axis=1)
        return {"pq": four(a["peer_w_q_2"][l]), "pk": lambda i: pad(k12.transpose(3, 0, 1, 2).reshape(P, -1))}

    made = {
        "zi": lambda i: feature_panel(wz, [tile(j) for j in range(4 * i, min(4 * i + 4, 7))]),
        "uq": lambda i: feature_panel(wu, [tile(6 * i + j) for j in range(6)]),
        "ukv": lambda i: pad(np.concatenate([
            feature_panel(wkv[:, :, :NOPE].reshape(KVL, -1), [tile(j) for j in range(8)])[:, :2048],
            token_panel(wkv[:, :, NOPE:].reshape(KVL, -1))[:, :2048]], axis=1)),
        "wo": four(a["mla_w_o_2"][0]), **peer(0)}
    panels += [made[s](i) for s, i in B_PANELS]
    grp = a["pool_w_grp_2"][0]
    made = {
        "pin": four(a["pool_w_in_2"][0]), "pout": four(a["pool_w_out_2"][0]),
        "grp": lambda i: pad(np.concatenate([feature_panel(grp[j // 2], [tile(j % 2)])[:, :2 * P] for j in range(8)],
                                            axis=1)), **peer(1)}
    panels += [made[s](i) for s, i in C_PANELS]

    vec_a = np.stack([np.concatenate(
        [by_partition(a[n][l]) for n in ("ln1_g", "ln1_b", "ln2_g", "ln2_b", "ln3_g", "ln3_b")]
        + [a["conv_w"][l].T.reshape(CF, P, TAPS).transpose(1, 0, 2).reshape(P, -1)]
        + [by_partition(a[n][l]) for n in ("conv_b", "conv_ln_g", "conv_ln_b", "gla_norm_g", "b_a")]
        + [a["w_in"][l][:, cuts[6]:].reshape(KD, P, RANK).transpose(1, 0, 2).reshape(P, -1)]
        + [np.pad(a["w_a2"][l], ((0, P - RANK), (0, 0)))]
        + [by_partition(a["b_mod_2"][l])], axis=1) for l in range(DEPTH)])
    vec_b = np.concatenate([by_partition(a["ln0_g"]), by_partition(a["ln0_b"]),
                            by_partition(a["ln_g_2"]), by_partition(a["ln_b_2"]),
                            by_partition(a["mla_q_norm_2"][0]), by_partition(a["mla_kv_norm_2"][0]),
                            by_partition(a["pool_scale_2"][0])], axis=1)
    acts = np.stack([feature_major(a["x"][0]), feature_major(a["mem"][0]), feature_major(a["ctx_2"][0])])
    return {"panels": np.stack(panels), "vec_a": vec_a, "vec_b": vec_b, "consts": shape_constants(),
            "mask": causal_mask(), "acts": acts,
            "tables": np.concatenate([a["peer_u_2"], a["peer_v_2"]], axis=2).reshape(DEPTH * NEXP, 2 * D),
            "c_rows": np.tile(np.concatenate([a["c_2"][0], a["c_ctx_2"]]), (P, 1))}


def causal_mask():
    s, c = np.arange(P)[:, None], np.arange(P)[None, :]
    return ((s <= c) & (s // CHUNK == c // CHUNK)).astype(np.uint32)


def shape_constants():
    n_freq, grid = ROPE // 4, 64
    t = np.arange(T)
    freqs = (np.float32(10000.0) ** (-np.arange(n_freq, dtype=np.float32) / n_freq)).astype(np.float32)
    ang = np.concatenate([(t // grid).astype(np.float32)[:, None] * freqs,
                          (t % grid).astype(np.float32)[:, None] * freqs], axis=1).astype(np.float32)
    cos = np.concatenate([np.tile(np.cos(ang).T, (4, 1)), np.ones((P, T), np.float32)], axis=1)
    sin = np.concatenate([np.tile(np.sin(ang).T, (4, 1)), np.zeros((P, T), np.float32)], axis=1)
    scan = np.tile((t % CHUNK != 0).astype(np.float32), (P, 1))
    count = [np.clip(t + w // 2, 0, T) - np.clip(t - w // 2, 0, T) for w in WINDOWS]
    inv = np.tile((1.0 / np.concatenate(count)).astype(np.float32), (P, 1))
    iota = np.tile(np.arange(TOPK, dtype=np.float32), (P, 1))
    return np.concatenate([np.eye(P, dtype=np.float32), cos, sin, scan, iota, inv], axis=1).astype(np.float32)


def kernel(**inputs):
    import concourse.bacc as bacc
    from concourse.bass_utils import run_bass_kernel_spmd

    arrays = {n: np.ascontiguousarray(x) for n, x in lay_out({n: np.asarray(x) for n, x in inputs.items()}).items()}
    nc = bacc.Bacc("TRN2", target_bir_lowering=False, num_devices=1)
    aps = [nc.dram_tensor(n, x.shape, mybir.dt.from_np(x.dtype), kind="ExternalInput").ap() for n, x in arrays.items()]
    out = nc.dram_tensor("out", (P, KD * T), F32, kind="ExternalOutput").ap()
    build_program(nc, *aps, out)
    got = run_bass_kernel_spmd(nc, [arrays], core_ids=[0]).results[0]["out"]
    return got.reshape(P, KD, T).transpose(2, 1, 0).reshape(1, T, D)
```
